# Optimizing a Trainium2 kernel written in Bass

```python
import math
import jax, jax.numpy as jnp
from jax import lax
import numpy as np

D_MODEL = 1024
BATCH = 1
SEQ = 512
DEPTH = 2

MEM_LEN = 256
N_MIXERS = 2
N_A = (DEPTH + N_MIXERS - 1) // N_MIXERS
N_B = DEPTH // N_MIXERS
ROPE_THETA = 10000.0
NORM_EPS = 1e-6
DA_HEADS = D_MODEL // 128
DA_QK_DIM = 64
DA_V_DIM = 2 * DA_QK_DIM
DA_Q_BLOCK = 128
DB_PAIRS = ((128, 1), (512, 4), (2048, 16))
DB_SLOTS = 8
DB_HEAD_DIM = 128
DB_Q_BLOCK = 64
XA_HEADS = 4
XA_HEAD_DIM = D_MODEL // XA_HEADS
D_FF = 4 * D_MODEL

kernel_name = 'hybrid_diff_dilated_encoder'

def rms_norm(x, g):
    xf = x.astype(jnp.float32)
    y = xf * lax.rsqrt(jnp.mean(xf * xf, axis=-1, keepdims=True) + NORM_EPS)
    return (y * g.astype(jnp.float32)).astype(x.dtype)

def rope(t, positions):
    dh = t.shape[-1]
    inv = ROPE_THETA ** (-jnp.arange(0, dh, 2, dtype=jnp.float32) / dh)
    ang = positions.astype(jnp.float32)[..., None] * inv
    ang = ang.reshape(ang.shape[:2] + (1,) * (t.ndim - 3) + (dh // 2,))
    cos, sin = jnp.cos(ang), jnp.sin(ang)
    tf = t.astype(jnp.float32)
    t1, t2 = tf[..., : dh // 2], tf[..., dh // 2:]
    return jnp.concatenate([t1 * cos - t2 * sin, t1 * sin + t2 * cos], axis=-1).astype(t.dtype)

def diff_attention(h, positions, w_qkv, lam, subln_g, w_o, lambda_init):
    B, S, _ = h.shape
    H, dq, dv = DA_HEADS, DA_QK_DIM, DA_V_DIM
    qkv = h @ w_qkv
    q, k, v = jnp.split(qkv, [H * 2 * dq, 2 * H * 2 * dq], axis=-1)
    q = rope(q.reshape(B, S, H, 2, dq), positions)
    k = rope(k.reshape(B, S, H, 2, dq), positions)
    v = v.reshape(B, S, H, dv)
    lamf = lam.astype(jnp.float32)
    lam_full = jnp.exp(jnp.sum(lamf[0] * lamf[1])) - jnp.exp(jnp.sum(lamf[2] * lamf[3])) + lambda_init
    nblk = S // DA_Q_BLOCK
    qb = q.reshape(B, nblk, DA_Q_BLOCK, H, 2, dq).transpose(1, 0, 2, 3, 4, 5)
    scale = dq ** -0.5

    def block(qi):
        s = jnp.einsum('bqhcd,bkhcd->bhcqk', qi, k).astype(jnp.float32) * scale
        p = jax.nn.softmax(s, axis=-1)
        a = (p[:, :, 0] - lam_full * p[:, :, 1]).astype(v.dtype)
        return jnp.einsum('bhqk,bkhd->bqhd', a, v)

    o = lax.map(block, qb)
    o = o.transpose(1, 0, 2, 3, 4).reshape(B, S, H, dv)
    o = rms_norm(o, subln_g) * (1.0 - lambda_init)
    return o.reshape(B, S, H * dv) @ w_o

def banded_attention(q, k, v, radius):
    N, L, H, Dh = q.shape
    QB = DB_Q_BLOCK
    nb = -(-L // QB)
    Lp = nb * QB
    KB = QB + 2 * radius
    q = jnp.pad(q, ((0, 0), (0, Lp - L), (0, 0), (0, 0)))
    kpad = ((0, 0), (radius, Lp - L + radius), (0, 0), (0, 0))
    k = jnp.pad(k, kpad)
    v = jnp.pad(v, kpad)
    idx = (jnp.arange(nb) * QB)[:, None] + jnp.arange(KB)[None, :]
    kb = k[:, idx]
    vb = v[:, idx]
    qb = q.reshape(N, nb, QB, H, Dh)
    rel = jnp.arange(KB)[None, :] - radius - jnp.arange(QB)[:, None]
    key_pos = idx - radius
    mask = (jnp.abs(rel) <= radius)[None] & ((key_pos >= 0) & (key_pos < L))[:, None, :]
    s = jnp.einsum('nbqhd,nbkhd->nbhqk', qb, kb).astype(jnp.float32) * (Dh ** -0.5)
    s = jnp.where(mask[None, :, None], s, -jnp.inf)
    m = jnp.max(s, axis=-1, keepdims=True)
    p = jnp.exp(s - m)
    den = jnp.sum(p, axis=-1, keepdims=True)
    o = jnp.einsum('nbhqk,nbkhd->nbqhd', (p / den).astype(v.dtype), vb)
    lse = (m + jnp.log(den))[..., 0]
    o = o.reshape(N, Lp, H, Dh)[:, :L]
    lse = lse.transpose(0, 1, 3, 2).reshape(N, Lp, H)[:, :L]
    return o, lse

def dilated_group(q, k, v, dilation, radius):
    B, S, H, Dh = q.shape
    L = S // dilation

    def split(t):
        return t.reshape(B, L, dilation, H, Dh).transpose(0, 2, 1, 3, 4).reshape(B * dilation, L, H, Dh)

    o, lse = banded_attention(split(q), split(k), split(v), radius)
    o = o.reshape(B, dilation, L, H, Dh).transpose(0, 2, 1, 3, 4).reshape(B, S, H, Dh)
    lse = lse.reshape(B, dilation, L, H).transpose(0, 2, 1, 3).reshape(B, S, H)
    return o, lse

def dilated_attention(h, positions, w_qkv, w_o):
    B, S, _ = h.shape
    G, H, Dh = len(DB_PAIRS), DB_SLOTS, DB_HEAD_DIM
    qkv = (h @ w_qkv).reshape(B, S, 3, G, H, Dh)
    q = rope(qkv[:, :, 0], positions)
    k = rope(qkv[:, :, 1], positions)
    v = qkv[:, :, 2]
    outs, lses = [], []
    for g, (window, dil) in enumerate(DB_PAIRS):
        o, lse = dilated_group(q[:, :, g], k[:, :, g], v[:, :, g], dil, (window // 2) // dil)
        outs.append(o)
        lses.append(lse)
    wts = jax.nn.softmax(jnp.stack(lses), axis=0)
    o = jnp.einsum('gbsh,gbshd->bshd', wts, jnp.stack(outs).astype(jnp.float32)).astype(h.dtype)
    return o.reshape(B, S, H * Dh) @ w_o

def memory_cross_attention(h, mem, mem_g, wq, wkv, wo):
    B, S, _ = h.shape
    H, Dh = XA_HEADS, XA_HEAD_DIM
    M = mem.shape[1]
    mn = rms_norm(mem, mem_g)
    q = (h @ wq).reshape(B, S, H, Dh)
    kv = (mn @ wkv).reshape(B, M, 2, H, Dh)
    s = jnp.einsum('bqhd,bkhd->bhqk', q, kv[:, :, 0]).astype(jnp.float32) * (Dh ** -0.5)
    p = jax.nn.softmax(s, axis=-1).astype(h.dtype)
    o = jnp.einsum('bhqk,bkhd->bqhd', p, kv[:, :, 1])
    return o.reshape(B, S, H * Dh) @ wo

def squared_relu_mlp(h, w_up, w_down):
    return jnp.square(jax.nn.relu(h @ w_up)) @ w_down

def setup_inputs(seed: int = 0) -> dict:
    key = jax.random.key(seed)
    ks = jax.random.split(key, 24)

    def gain(k, shape):
        return 1.0 + 0.05 * jax.random.normal(k, shape, jnp.float32)

    def weight(k, shape, fan_in):
        return jax.random.normal(k, shape, jnp.float32) * (fan_in ** -0.5)

    D = D_MODEL
    da_w = DA_HEADS * DA_V_DIM
    db_w = len(DB_PAIRS) * DB_SLOTS * DB_HEAD_DIM
    xa_w = XA_HEADS * XA_HEAD_DIM
    x = jax.random.normal(ks[0], (BATCH, SEQ, D), jnp.float32)
    mem = jax.random.normal(ks[1], (BATCH, MEM_LEN, D), jnp.float32)
    positions = (jnp.arange(SEQ, dtype=jnp.int32)[None, :]
                 + jax.random.randint(ks[2], (BATCH, 1), 0, 1024, dtype=jnp.int32))
    return {
        'x': x,
        'mem': mem,
        'positions': positions,
        'mix_pre_g': gain(ks[3], (DEPTH, D)),
        'mix_post_g': gain(ks[4], (DEPTH, D)),
        'da_w_qkv': weight(ks[5], (N_A, D, 3 * da_w), D),
        'da_lambda': 0.1 * jax.random.normal(ks[6], (N_A, 4, DA_QK_DIM), jnp.float32),
        'da_subln_g': gain(ks[7], (N_A, DA_V_DIM)),
        'da_w_o': weight(ks[8], (N_A, da_w, D), da_w),
        'db_w_qkv': weight(ks[9], (N_B, D, 3 * db_w), D),
        'db_w_o': weight(ks[10], (N_B, DB_SLOTS * DB_HEAD_DIM, D), DB_SLOTS * DB_HEAD_DIM),
        'xa_pre_g': gain(ks[11], (DEPTH, D)),
        'mem_g': gain(ks[12], (DEPTH, D)),
        'xa_wq': weight(ks[13], (DEPTH, D, xa_w), D),
        'xa_wkv': weight(ks[14], (DEPTH, D, 2 * xa_w), D),
        'xa_wo': weight(ks[15], (DEPTH, xa_w, D), xa_w),
        'xa_post_g': gain(ks[16], (DEPTH, D)),
        'ffn_pre_g': gain(ks[17], (DEPTH, D)),
        'w_up': weight(ks[18], (DEPTH, D, D_FF), D),
        'w_down': weight(ks[19], (DEPTH, D_FF, D), D_FF),
        'ffn_post_g': gain(ks[20], (DEPTH, D)),
    }

def reference(x, mem, positions, mix_pre_g, mix_post_g, da_w_qkv, da_lambda, da_subln_g, da_w_o,
              db_w_qkv, db_w_o, xa_pre_g, mem_g, xa_wq, xa_wkv, xa_wo, xa_post_g,
              ffn_pre_g, w_up, w_down, ffn_post_g):
    for i in range(DEPTH):
        j = i // N_MIXERS
        h = rms_norm(x, mix_pre_g[i])
        if i % N_MIXERS == 0:
            lambda_init = 0.8 - 0.6 * math.exp(-0.3 * i)
            mix = diff_attention(h, positions, da_w_qkv[j], da_lambda[j], da_subln_g[j], da_w_o[j], lambda_init)
        else:
            mix = dilated_attention(h, positions, db_w_qkv[j], db_w_o[j])
        x = x + rms_norm(mix, mix_post_g[i])
        h = rms_norm(x, xa_pre_g[i])
        x = x + rms_norm(memory_cross_attention(h, mem, mem_g[i], xa_wq[i], xa_wkv[i], xa_wo[i]), xa_post_g[i])
        h = rms_norm(x, ffn_pre_g[i])
        x = x + rms_norm(squared_relu_mlp(h, w_up[i], w_down[i]), ffn_post_g[i])
    return x


_drawn_inputs = setup_inputs


def setup_inputs(seed=0):
    import zlib

    import numpy as np

    out = dict(_drawn_inputs(seed))
    spreads = {}
    factors = {}
    for name, (base, spread) in spreads.items():
        noise = np.random.default_rng([zlib.crc32(name.encode()), seed]).standard_normal(out[name].shape)
        drawn = base * np.exp(spread * noise) if base else spread * noise
        out[name] = __import__('jax').numpy.asarray(drawn.astype(out[name].dtype))
    for name, factor in factors.items():
        out[name] = (out[name] * factor).astype(out[name].dtype)
    return out
```

```python
import math
from contextlib import ExitStack

import numpy as np

import concourse.bass as bass
from concourse import mybir

D = 1024
S = 512
MEM = 256
P = 128
KT = D // P
NB = 512
EPS = 1e-6
THETA = 10000.0
DA_HEADS, DA_DQ = 8, 64
LAMBDA_INIT = 0.8 - 0.6 * math.exp(-0.3 * 0)
GROUPS, DB_DH = 3, 128
HALF = 4
DIL = 4
RADIUS = 64
XA_HEADS, XA_DH = 4, 256
XB = XA_DH // P
FF = 4 * D
CHUNKS = FF // D
MASKED = -1.0e37
LAYER_GAINS = ["mix_pre_g", "mix_post_g", "xa_pre_g", "mem_g", "xa_post_g", "ffn_pre_g", "ffn_post_g"]

C_INV0, C_SIGN0, C_INV1, C_SIGN1 = range(4)


def rope_columns():
    cols = np.zeros((P, 4), np.float32)
    for at, dh in ((0, DA_DQ), (2, DB_DH)):
        inv = np.float32(THETA) ** (-np.arange(0, dh, 2, dtype=np.float32) / np.float32(dh))
        row = np.arange(P) % dh
        cols[:, at] = inv.astype(np.float32)[row % (dh // 2)]
        cols[:, at + 1] = np.where(row < dh // 2, 1.0, -1.0)
    return cols


def two_pi_parts():
    parts, rest = [], 2 * math.pi
    for bits in (8, 9, 9):
        e = math.floor(math.log2(rest)) - bits + 1
        part = math.floor(rest / 2.0**e) * 2.0**e
        parts.append(part)
        rest -= part
    return parts + [rest]


def numbered(names, sizes):
    at, n = {}, 0
    for name, size in zip(names, sizes):
        at[name] = n
        n += size
    return at, n


UNITS, TOTAL_UNITS = numbered(
    ["qkv0", "o0", "kv0", "xq0", "xo0", "ff0", "qkv1a", "qkv1b", "o1", "kv1", "xq1", "xo1", "ff1"],
    [6, 2, 4, 2, 2, 4 * CHUNKS, 3 * GROUPS, 3 * GROUPS, 2, 4, 2, 2, 4 * CHUNKS])
SPLIT_NAMES = ["pre0", "o0", "mem0", "xpre0", "xo0", "fpre0", "ff0", "pre1", "o1", "mem1", "xpre1", "xo1",
               "fpre1", "ff1"]
SPLITS, _ = numbered(SPLIT_NAMES, [KT * CHUNKS if n.startswith("ff") else KT for n in SPLIT_NAMES])
STAGED_NAMES = [n for n in SPLIT_NAMES if n not in ("xo0", "o1", "xo1")]
STAGED, _ = numbered(STAGED_NAMES, [KT * CHUNKS if n.startswith("ff") else KT for n in STAGED_NAMES])
STAT_NAMES = ["pre0", "mem0", "mix0", "xpre0", "xa0", "fpre0", "ff0",
              "pre1", "mem1", "mix1", "xpre1", "xa1", "fpre1", "ff1"]
STATS, _ = numbered(STAT_NAMES, [1] * len(STAT_NAMES))
STAT_BEFORE = {"pre0": UNITS["qkv0"], "ff0": UNITS["qkv1a"], "pre1": UNITS["qkv1a"], "ff1": TOTAL_UNITS}
for _l in "01":
    STAT_BEFORE.update({"mem" + _l: UNITS["o" + _l] + 1, "mix" + _l: UNITS["kv" + _l] + 1,
                        "xpre" + _l: UNITS["kv" + _l] + 2, "xa" + _l: UNITS["ff" + _l],
                        "fpre" + _l: UNITS["ff" + _l]})


def stat_bank(name):
    return 4 * (STAT_BEFORE[name] % 2) + 3


def banks_out(u, m, ii=0, nb=4):
    return ii * 4 + (4 * (u // 2) + (m + 1) * (4 // nb))


def residue(ap, r):
    return ap.rearrange("p (l r) -> p r l", r=DIL)[:, r]


def build(nc, x, mem, positions, gains, consts, lam, subln_g, da_w_qkv, da_w_o, db_w_qkv, db_w_o,
          xa_wq, xa_wkv, xa_wo, w_up, w_down, out):
    f32, f32r, bf16, i32 = mybir.dt.float32, mybir.dt.float32r, mybir.dt.bfloat16, mybir.dt.int32
    ACT = mybir.ActivationFunctionType
    ALU = mybir.AluOpType
    AX = mybir.AxisListType

    def tiles(w):
        return w.rearrange("(r a p) (n c) -> r n p a c", a=2, p=P, c=NB)

    with ExitStack() as ctx:
        def sb(name, shape, dt=f32, scope=ctx):
            return scope.enter_context(nc.sbuf_tensor(name, shape, dt))

        def sem(name):
            return ctx.enter_context(nc.semaphore(name))

        x_sb = sb("x_sb", [P, KT, S])
        y_sb = sb("y_sb", [P, KT, S])
        act_hi = sb("act_hi", [P, KT, S], f32r)
        act_lo = sb("act_lo", [P, KT, S], f32r)
        raw = sb("raw", [P, 4, 2, NB])
        w_hi = sb("w_hi", [P, 2, 2, NB], f32r)
        w_lo = sb("w_lo", [P, 2, 2, NB], f32r)
        cos_sb = sb("cos_sb", [P, 1, S])
        sin_sb = sb("sin_sb", [P, 1, S])
        posf = sb("posf", [P, S])
        mask = sb("mask", [P, DIL, S + 2 * P], bf16)
        stage = sb("stage", [P, 2, S])
        half = sb("half", [P, 2, S])
        rstd = sb("rstd", [P, S])
        gain = sb("gain", [P, 2 * len(LAYER_GAINS), KT])
        cst = sb("cst", [P, 4])
        lam_sb = half[:, 1, 0:4 * DA_DQ].rearrange("p (a b) -> p a b", a=4)
        lam_w = sb("lam_w", [P, 8])
        subg = sb("subg", [P, 2])
        ones = sb("ones", [P, P])
        ident = sb("ident", [P, P])
        phase4 = sb("phase4", [P, DIL])
        eps = sb("eps", [P, 1])
        small = sb("small", [P, 2, 8])
        with ExitStack() as scope:
            e_sb = sb("e_sb", [P, 2, 1024], scope=scope)
            pT_sb = sb("pT_sb", [P, 2, 768], scope=scope)
        sq = sb("sq", [P, KT, S])
        with ExitStack() as scope:
            q0 = sb("q0", [P, DA_HEADS, S], scope=scope)
            k0 = sb("k0", [P, DA_HEADS, S], scope=scope)
            v0 = sb("v0", [P, S // P, D], scope=scope)
        with ExitStack() as scope:
            q1 = sb("q1", [P, GROUPS, HALF, S], scope=scope)
            k1 = sb("k1", [P, GROUPS, HALF, S], scope=scope)
            v1 = sb("v1", [P, GROUPS, S // P, HALF * P], scope=scope)
        with ExitStack() as scope:
            xq = sb("xq", [P, KT, S], scope=scope)
            xk = sb("xk", [P, KT, MEM], scope=scope)
            xv = sb("xv", [P, MEM // P, D], scope=scope)
            mem_sb = sb("mem_sb", [P, KT, MEM], scope=scope)
            mem_hi = sb("mem_hi", [P, KT, MEM], f32r, scope=scope)
            mem_lo = sb("mem_lo", [P, KT, MEM], f32r, scope=scope)
        with ExitStack() as scope:
            ff_hi = sb("ff_hi", [P, KT, S], f32r, scope=scope)
            ff_lo = sb("ff_lo", [P, KT, S], f32r, scope=scope)
        ps = ctx.enter_context(nc.psum_tensor("ps", [P, 8, NB], f32))

        raw_loaded = [sem(f"raw_loaded{j}") for j in range(4)]
        w_hi_ready = sem("w_hi_ready")
        w_lo_ready = sem("w_lo_ready")
        pair_used = sem("pair_used")
        bank_done = sem("bank_done")
        bank_out = [sem("bank_out0"), sem("bank_out1")]
        hi_ready = sem("hi_ready")
        lo_ready = sem("lo_ready")
        staged = sem("staged")
        sq_ready = sem("sq_ready")
        stat_done = sem("stat_done")
        ln_done = sem("ln_done")
        rstd_ready = sem("rstd_ready")
        y_scaled = sem("y_scaled")
        x_ready = sem("x_ready")
        y_cleared = sem("y_cleared")
        rope_done = sem("rope_done")
        sub_sq = sem("sub_sq")
        sub_stat = sem("sub_stat")
        sub_ln = sem("sub_ln")
        sub_rstd = sem("sub_rstd")
        x_loaded = sem("x_loaded")
        small_loaded = sem("small_loaded")
        mem_loaded = sem("mem_loaded")
        dve_step = sem("dve_step")
        constants = sem("constants")
        phase_ready = sem("phase_ready")
        mask_step = sem("mask_step")
        angles = sem("angles")
        tables = sem("tables")
        lam_sums = sem("lam_sums")
        lam_exp = sem("lam_exp")
        out_done = sem("out_done")

        class Attention:

            def __init__(self, name, heads, blocks, wide=False):
                self.heads, self.steps, self.blocks = heads, S // P, blocks
                self.wide = wide
                self.n = heads * self.steps
                self.scores = sem(name + "_scores")
                self.taken = sem(name + "_taken")
                self.exps = sem(name + "_exps")
                self.probs = sem(name + "_probs")
                self.mid = sem(name + "_mid")
                self.turned = sem(name + "_turned")
                self.pT = sem(name + "_pT")
                self.weighed = sem(name + "_weighed")
                self.o_out = sem(name + "_o_out")

            def turn_banks(self, n, b):
                if self.wide:
                    return ps[:, 4 + b // 4, (b % 4) * P:(b % 4 + 1) * P]
                return ps[:, 4 + n % 2, b * P:(b + 1) * P]

            def turned_all(self, n):
                if self.wide:
                    return ps[:, 4:6, :].rearrange("p b c -> p (b c)")[:, 0:self.blocks * P]
                return ps[:, 4 + n % 2, 0:self.blocks * P]

        att_d = Attention("diff", DA_HEADS, S // P)
        att_l = [Attention(f"dil{h}", HALF, S // P + 2, wide=True) for h in range(2)]
        att_x = [Attention(f"cross{i}", XA_HEADS, MEM // P) for i in range(2)]

        def gcol(layer, name, k):
            n = layer * len(LAYER_GAINS) + LAYER_GAINS.index(name)
            return gain[:, n, k:k + 1]

        block = ctx.enter_context(nc.Block())

        @block.sync
        def _(sp):
            def load_unit(u, w, row_pair, col, ii=0):
                for j in range(4):
                    if u > 0:
                        sp.wait_ge(w_lo_ready, ii * 8 + (4 * u + j - 3))
                    src = w[bass.ds(row_pair + j, 1), bass.ds(col, 1)]
                    sp.dma_start(raw[:, j], src[0, 0]).then_inc(raw_loaded[j], 16)

            for k in range(0, KT, 2):
                sp.dma_start(x_sb[:, k:k + 2, :], x[:, k:k + 2]).then_inc(x_loaded, 16)
            w = tiles(da_w_qkv)
            load_unit(0, w, 0, 0)
            sp.dma_start(gain[:, :, :], gains).then_inc(small_loaded, 16)
            sp.dma_start(cst[:, :], consts).then_inc(small_loaded, 16)
            sp.dma_start(half[:, 0, :].bitcast(i32), positions.broadcast_to([P, S])).then_inc(small_loaded, 16)
            sp.dma_start(half[:, 1, 0:4 * DA_DQ],
                         lam.broadcast_to([P, 4 * DA_DQ])).then_inc(small_loaded, 16)
            sp.dma_start(subg[:, 0:1], subln_g).then_inc(small_loaded, 16)
            for n in range(1, 6):
                load_unit(n, w, 0, n)

            def after_attention(layer, att):
                u = UNITS[f"o{layer}"]
                w = tiles(da_w_o if layer == 0 else db_w_o)
                load_unit(u, w, 0, 0)
                sp.wait_ge(att.weighed, att.n)
                sp.dma_start(mem_sb[:, :, :], mem).then_inc(mem_loaded, 16)
                load_unit(u + 1, w, 0, 1)
                w = tiles(xa_wkv[layer])
                for n, col in enumerate((2, 3, 0, 1)):
                    load_unit(UNITS[f"kv{layer}"] + n, w, 0, col)
                for name, w in (("xq", xa_wq), ("xo", xa_wo)):
                    for n in range(2):
                        load_unit(UNITS[f"{name}{layer}"] + n, tiles(w[layer]), 0, n)
                u = UNITS[f"ff{layer}"]
                up, down = tiles(w_up[layer]), tiles(w_down[layer])
                with sp.Fori(0, CHUNKS) as c:
                    for n in range(2):
                        load_unit(u + n, up, 0, c * 2 + n, c * 2)
                    for n in range(2):
                        load_unit(u + 2 + n, down, c * 4, n, c * 2)

            after_attention(0, att_d)
            w = tiles(db_w_qkv)
            for h in range(2):
                u = UNITS["qkv1a" if h == 0 else "qkv1b"]
                with sp.Fori(0, GROUPS) as g:
                    load_unit(u, w, 0, g * 2 + h, g)
                    load_unit(u + 1, w, 0, g * 2 + (2 * GROUPS + h), g)
                for g in range(GROUPS):
                    load_unit(u + 2 * GROUPS + g, w, 0, 4 * GROUPS + 2 * g + h)
            after_attention(1, att_l[1])
            for k in range(KT):
                sp.wait_ge(x_ready, 5 * KT + k + 1)
                sp.dma_start(out[:, k], x_sb[:, k, :]).then_inc(out_done, 16)
            sp.wait_ge(out_done, 16 * KT)

        @block.gpsimd
        def _(pool):
            nc.gpsimd.memset(ones[:, :], 1.0).then_inc(constants, 1)
            nc.gpsimd.memset(eps[:, :], EPS).then_inc(constants, 1)
            nc.gpsimd.memset(ident[:, :], 0.0).then_inc(constants, 1)
            pool.wait_ge(constants, 3)
            nc.gpsimd.affine_select(out=ident[:, :], in_=ident[:, :], compare_op=ALU.not_equal, fill=1.0,
                                    base=0, pattern=[[-1, P]], channel_multiplier=1).then_inc(constants, 1)

            nc.gpsimd.memset(mask[:, :, 0:S + P], 0.0).then_inc(mask_step, 1)
            steps = 1
            for r in range(DIL):
                for at, width, step, base in ((0, S, DIL, r), (S, P, 1, 0)):
                    part = mask[:, r, at:at + width]
                    for sign in (1, -1):
                        pool.wait_ge(mask_step, steps)
                        nc.gpsimd.affine_select(out=part, in_=part, compare_op=ALU.is_ge, fill=MASKED,
                                                base=RADIUS - sign * base, pattern=[[sign, width]],
                                                channel_multiplier=-sign * step).then_inc(mask_step, 1)
                        steps += 1
                if r == 0:
                    pool.wait_ge(phase_ready, 1)
                for a in range(2):
                    far = mask[:, r, S + P + a * 64:S + P + (a + 1) * 64].rearrange("p (a b) -> p a b", b=DIL)
                    nc.gpsimd.tensor_copy(far, phase4[:, :].rearrange("p (o b) -> p o b", o=1)
                                          .broadcast_to([P, 16, DIL])).then_inc(mask_step, 1)
                    steps += 1
            assert steps == MASK_STEPS

            def rope_sum(value, parity, dst, n):
                pool.wait_ge(bank_out[parity], value)
                nc.gpsimd.tensor_tensor(dst, dst, half[:, n % 2:n % 2 + 1, :], ALU.add).then_inc(rope_done, 1)

            for n in range(16):
                u = UNITS["qkv0"] + n // 4
                dst = (q0 if n < 8 else k0)[:, n % 8:n % 8 + 1, :]
                rope_sum(banks_out(u, n % 4), u % 2, dst, n)
            for layer in range(2):
                pool.wait_ge(x_ready, KT * (3 * layer + 2))
                nc.gpsimd.memset(y_sb[:, :, :], 0.0).then_inc(y_cleared, 1)
                if layer == 0:
                    for name in ("qkv1a", "qkv1b"):
                        u = UNITS[name]
                        with pool.Fori(0, GROUPS) as g:
                            for kind, dst in enumerate((q1, k1)):
                                for m in range(HALF):
                                    rope_sum(banks_out(u + kind, m, g), (u + kind) % 2,
                                             dst[:, bass.ds(g, 1), m, :], m)

        @block.scalar
        def _(act):
            def heads_of(g, ii=0):
                act.wait_ge(raw_loaded[g % 4], ii * 32 + 16 * (g // 4 + 1))
                if g >= 2:
                    v, j = divmod(g - 2, 4)
                    if j < 3:
                        act.wait_ge(pair_used, ii * 6 + (3 * v + j + 1))
                    else:
                        act.wait_ge(bank_done, ii * 8 + 4 * (v + 1))
                nc.scalar.activation(w_hi[:, g % 2], raw[:, g % 4], ACT.Copy).then_inc(w_hi_ready, 1)

            def unit(u, bank=None, ii=0, nb=4):
                heads_of(4 * u + 2, ii)
                heads_of(4 * u + 3, ii)
                for m in range(4):
                    if m % 2 == 0 and u + 1 < TOTAL_UNITS:
                        heads_of(4 * u + 4 + m // 2, ii)
                    if bank and m < nb:
                        bank(m)

            def copies(u, dst, nb=4, width=NB):
                def bank(m):
                    act.wait_ge(bank_done, 4 * u + (m + 1) * (4 // nb))
                    nc.scalar.activation(dst(m), ps[:, 4 * (u % 2) + m, 0:width],
                                         ACT.Copy).then_inc(bank_out[u % 2], 4 // nb)
                unit(u, bank, nb=nb)

            def squares(source, width=S, wait=None):
                for k in range(KT):
                    if wait:
                        wait(k)
                    nc.scalar.activation(sq[:, k, 0:width], source[:, k, :], ACT.Square).then_inc(sq_ready, 1)

            def y_is_out(u):
                return lambda k: act.wait_ge(bank_out[(u + k // 4) % 2], banks_out(u + k // 4, k % 4))

            def x_is_new(post):
                return lambda k: act.wait_ge(x_ready, KT * post + k + 1)

            def root(name, width=S):
                n = STATS[name]
                act.wait_ge(stat_done, n + 1)
                nc.scalar.activation(rstd[:, 0:width], ps[:, stat_bank(name), 0:width], ACT.Ln,
                                     bias=eps[:, 0:1], scale=1.0 / D).then_inc(ln_done, 1)
                act.wait_ge(ln_done, n + 1)
                nc.scalar.activation(rstd[:, 0:width], rstd[:, 0:width], ACT.Exp,
                                     scale=-0.5).then_inc(rstd_ready, 1)

            def staged_heads(name, dst, width=S):
                for k in range(KT):
                    act.wait_ge(staged, STAGED[name] + k + 1)
                    nc.scalar.activation(dst[:, k, :], stage[:, k % 2, 0:width], ACT.Copy).then_inc(hi_ready, 1)

            def sines(layer):
                act.wait_ge(angles, 2 * layer + 1)
                s = C_SIGN1 if layer else C_SIGN0
                nc.scalar.activation(sin_sb[:, 0, :], sq[:, 2, :], ACT.Sin, scale=cst[:, s:s + 1]).then_inc(tables, 1)
                act.wait_ge(angles, 2 * layer + 2)
                nc.scalar.activation(cos_sb[:, 0, :], sq[:, 3, :], ACT.Sin).then_inc(tables, 1)
                nc.scalar.preload_act_table_set("natural_log_exp_and_others")

            def attention(a, exp, head_out):
                for t in range(a.n + 2):
                    if t < a.n:
                        act.wait_ge(a.taken, t + 1)
                        if t >= 2:
                            act.wait_ge(a.turned, t - 1)
                        exp(a, t)
                    if 1 <= t <= a.n:
                        n = t - 1
                        act.wait_ge(a.turned, n + 1)
                        if n >= 2:
                            act.wait_ge(a.weighed, n - 1)
                        nc.scalar.activation(pT_sb[:, n % 2, 0:a.blocks * P], a.turned_all(n),
                                             ACT.Copy).then_inc(a.pT, 1)
                    if t > a.steps and (t - 1) % a.steps == 0:
                        head_out(a, (t - 1) // a.steps - 1)

            def exp_diff(a, t):
                for c in range(2):
                    nc.scalar.activation(e_sb[:, t % 2, c * S:(c + 1) * S], ps[:, 2 * (t % 2) + c, :], ACT.Exp,
                                         bias=small[:, t % 2, 2 + c:3 + c], scale=DA_DQ ** -0.5,
                                         accum_out=small[:, t % 2, 4 + c:5 + c]).then_inc(a.exps, 1)

            def exp_cross(a, t):
                nc.scalar.activation(e_sb[:, t % 2, 0:MEM], ps[:, 2 * (t % 2), 0:MEM], ACT.Exp,
                                     bias=small[:, t % 2, 2:3], scale=XA_DH ** -0.5,
                                     accum_out=small[:, t % 2, 4:5]).then_inc(a.exps, 1)

            def exp_dilated(a, t):
                w = a.blocks * P
                nc.scalar.activation(e_sb[:, t % 2, 0:w], e_sb[:, t % 2, 0:w], ACT.Exp,
                                     bias=small[:, t % 2, 2:3],
                                     accum_out=small[:, t % 2, 4:5]).then_inc(a.exps, 1)

            def head_to_y(first, dilated):
                def head_out(a, h):
                    act.wait_ge(a.weighed, a.steps * (h + 1))
                    src, dst = ps[:, 6 + h % 2, :], y_sb[:, first + h, :]
                    if dilated:
                        src = src.rearrange("p (r l) -> p r l", r=DIL)
                        dst = dst.rearrange("p (l r) -> p r l", r=DIL)
                    nc.scalar.activation(dst, src, ACT.Copy).then_inc(a.o_out, 1)
                return head_out

            def head_split(a, h):
                act.wait_ge(a.weighed, a.steps * (h + 1))
                for b in range(XB):
                    nc.scalar.activation(act_hi[:, XB * h + b, :], ps[:, 6 + b, :], ACT.Copy).then_inc(hi_ready, 1)

            nc.scalar.preload_act_table_set("natural_log_exp_and_others")
            squares(x_sb, wait=lambda k: act.wait_ge(x_loaded, 16 * KT // 2))
            heads_of(0)
            heads_of(1)
            act.wait_ge(constants, 4)
            root("pre0")
            staged_heads("pre0", act_hi)
            act.wait_ge(lam_sums, 2)
            nc.scalar.activation(lam_w[:, 2:4], lam_w[:, 0:2], ACT.Exp).then_inc(lam_exp, 1)
            act.wait_ge(small_loaded, 80)
            sines(0)
            u = UNITS["qkv0"]
            for n in range(4):
                unit(u + n)
            for n in range(2):
                copies(u + 4 + n, lambda m, n=n: v0[:, m, n * NB:(n + 1) * NB])
            attention(att_d, exp_diff, head_to_y(0, False))

            for h in range(DA_HEADS):
                act.wait_ge(att_d.o_out, h + 1)
                nc.scalar.activation(sq[:, h, :], y_sb[:, h, :], ACT.Square).then_inc(sub_sq, 1)
            for h in range(DA_HEADS + 1):
                if h < DA_HEADS:
                    act.wait_ge(sub_stat, h + 1)
                    if h >= 2:
                        act.wait_ge(staged, STAGED["o0"] + h - 1)
                    nc.scalar.activation(half[:, h % 2, :], ps[:, 4 + h % 4, :], ACT.Ln, bias=eps[:, 0:1],
                                         scale=1.0 / P).then_inc(sub_ln, 1)
                    act.wait_ge(sub_ln, h + 1)
                    nc.scalar.activation(half[:, h % 2, :], half[:, h % 2, :], ACT.Exp,
                                         scale=-0.5).then_inc(sub_rstd, 1)
                if h >= 1:
                    act.wait_ge(staged, STAGED["o0"] + h)
                    nc.scalar.activation(act_hi[:, h - 1, :], stage[:, (h - 1) % 2, :],
                                         ACT.Copy).then_inc(hi_ready, 1)

            for layer in range(2):
                if layer == 1:
                    squares(x_sb, wait=x_is_new(2))
                    root("pre1")
                    staged_heads("pre1", act_hi)
                    sines(1)
                    for h in range(2):
                        u = UNITS["qkv1a" if h == 0 else "qkv1b"]
                        with act.Fori(0, GROUPS) as g:
                            unit(u, ii=g)
                            unit(u + 1, ii=g)
                        u += 2 * GROUPS
                        for g in range(GROUPS):
                            copies(u + g, lambda m, g=g: v1[:, g, m, :])
                        attention(att_l[h], exp_dilated, head_to_y(HALF * h, True))
                    act.wait_ge(att_l[0].o_out, HALF)
                    act.wait_ge(att_l[1].o_out, HALF)
                    for k in range(KT):
                        nc.scalar.activation(act_hi[:, k, :], y_sb[:, k, :], ACT.Copy).then_inc(hi_ready, 1)

                u = UNITS[f"o{layer}"]
                copies(u, lambda m: y_sb[:, m, :])
                squares(mem_sb, MEM, wait=lambda k: act.wait_ge(mem_loaded, 16 * (layer + 1)))
                root(f"mem{layer}", MEM)
                staged_heads(f"mem{layer}", mem_hi, MEM)
                copies(u + 1, lambda m: y_sb[:, 4 + m, :])
                squares(y_sb, wait=y_is_out(u))
                u = UNITS[f"kv{layer}"]
                copies(u, lambda m: xv[:, m, 0:NB], nb=2)
                root(f"mix{layer}")
                squares(x_sb, wait=x_is_new(3 * layer))
                copies(u + 1, lambda m: xv[:, m, NB:2 * NB], nb=2)
                root(f"xpre{layer}")
                staged_heads(f"xpre{layer}", act_hi)
                for n in range(2):
                    copies(u + 2 + n, lambda m, n=n: xk[:, 4 * n + m, :], width=MEM)
                for n in range(2):
                    copies(UNITS[f"xq{layer}"] + n, lambda m, n=n: xq[:, 4 * n + m, :])
                attention(att_x[layer], exp_cross, head_split)
                u = UNITS[f"xo{layer}"]
                for n in range(2):
                    copies(u + n, lambda m, n=n: y_sb[:, 4 * n + m, :])
                squares(y_sb, wait=y_is_out(u))
                root(f"xa{layer}")
                squares(x_sb, wait=x_is_new(3 * layer + 1))
                root(f"fpre{layer}")
                staged_heads(f"fpre{layer}", act_hi)

                u, first = UNITS[f"ff{layer}"], STAGED[f"ff{layer}"]

                def chunk(c):
                    def relu_of(up):
                        def bank(m):
                            n = 4 * up + m
                            act.wait_ge(bank_done, c * 16 + (4 * (u + up) + m + 1))
                            act.wait_ge(staged, c * KT + (first + n - 1))
                            nc.scalar.activation(half[:, n % 2, :], ps[:, 4 * ((u + up) % 2) + m, :],
                                                 ACT.Relu).then_inc(bank_out[(u + up) % 2], 1)
                            if n >= 1:
                                square_head(n - 1)
                        return bank

                    def square_head(n):
                        act.wait_ge(staged, c * KT + (first + n + 1))
                        nc.scalar.activation(ff_hi[:, n, :], stage[:, n % 2, :], ACT.Copy).then_inc(hi_ready, 1)

                    unit(u, relu_of(0), c * 2)
                    unit(u + 1, relu_of(1), c * 2)
                    square_head(KT - 1)
                    unit(u + 2, None, c * 2)

                with act.Fori(0, CHUNKS - 1) as c:
                    chunk(c)
                    unit(u + 3, None, c * 2)
                chunk(CHUNKS - 1)
                unit(u + 4 * CHUNKS - 1, None)
                squares(y_sb, wait=y_is_out(u + 4 * CHUNKS - 2))
                root(f"ff{layer}")

        @block.vector
        def _(dve):
            steps = 0

            def step(ins):
                nonlocal steps
                steps += 1
                ins.then_inc(dve_step, 1)
                dve.wait_ge(dve_step, steps)

            def rests_of(g, ii=0):
                dve.wait_ge(w_hi_ready, ii * 8 + (g + 1))
                nc.vector.tensor_tensor(w_lo[:, g % 2], raw[:, g % 4], w_hi[:, g % 2].bitcast(f32),
                                        ALU.subtract).then_inc(w_lo_ready, 1)

            def unit(u, bank=None, ii=0):
                rests_of(4 * u + 2, ii)
                rests_of(4 * u + 3, ii)
                for m in range(4):
                    if m % 2 == 0 and u + 1 < TOTAL_UNITS:
                        rests_of(4 * u + 4 + m // 2, ii)
                    if bank:
                        bank(m)

            def rope_banks(u, dst, n0, swap, ii=0):
                def bank(m):
                    src = ps[:, 4 * (u % 2) + m:4 * (u % 2) + m + 1, :]
                    dve.wait_ge(bank_done, ii * 8 + (4 * u + m + 1))
                    nc.vector.tensor_tensor(dst(m), src, cos_sb[:, :, :], ALU.mult)
                    if n0 + m >= 2:
                        dve.wait_ge(rope_done, ii * 8 + (n0 + m - 1))
                    for at in range(0, P, swap):
                        to = at ^ swap
                        last = nc.vector.tensor_tensor(half[to:to + swap, m % 2:m % 2 + 1, :],
                                                       src[at:at + swap], sin_sb[at:at + swap], ALU.mult)
                    last.then_inc(bank_out[u % 2], 1)
                unit(u, bank, ii)

            def rest(name, k, dst_lo, hi, source):
                dve.wait_ge(hi_ready, SPLITS[name] + k + 1)
                nc.vector.tensor_tensor(dst_lo, source, hi.bitcast(f32), ALU.subtract).then_inc(lo_ready, 1)

            def stage_free(name, k):
                n = SPLITS[name] + k - 1
                if n > 0:
                    dve.wait_ge(hi_ready, n)
                    dve.wait_ge(lo_ready, n)

            def normalise(name, source, layer, gains_name, dst_hi, dst_lo, width=S):
                dve.wait_ge(rstd_ready, STATS[name] + 1)
                for k in range(KT + 1):
                    if k < KT:
                        stage_free(name, k)
                        nc.vector.scalar_tensor_tensor(stage[:, k % 2, 0:width], source[:, k, :],
                                                       gcol(layer, gains_name, k), rstd[:, 0:width],
                                                       ALU.mult, ALU.mult).then_inc(staged, 1)
                    if k >= 1:
                        dve.wait_ge(staged, STAGED[name] + k)
                        rest(name, k - 1, dst_lo[:, k - 1, :], dst_hi[:, k - 1, :], stage[:, (k - 1) % 2, 0:width])

            def add_normalised(name, layer, gains_name, post):
                dve.wait_ge(rstd_ready, STATS[name] + 1)
                for k in range(KT + 1):
                    if k < KT:
                        nc.vector.scalar_tensor_tensor(y_sb[:, k, :], y_sb[:, k, :], gcol(layer, gains_name, k),
                                                       rstd[:, :], ALU.mult, ALU.mult).then_inc(y_scaled, 1)
                    if k >= 1:
                        dve.wait_ge(y_scaled, KT * post + k)
                        nc.vector.tensor_tensor(x_sb[:, k - 1, :], x_sb[:, k - 1, :], y_sb[:, k - 1, :],
                                                ALU.add).then_inc(x_ready, 1)

            def reduced_angles(layer):
                inv = C_INV1 if layer else C_INV0
                angle, turns, r = sq[:, 0, :], sq[:, 1, :], sq[:, 2, :]
                step(nc.vector.tensor_scalar(angle, posf[:, :], cst[:, inv:inv + 1], None, ALU.mult))
                step(nc.vector.tensor_scalar(turns, angle, 1.0 / (2 * math.pi), None, ALU.mult))
                step(nc.vector.tensor_scalar(turns, turns, 12582912.0, None, ALU.add))
                step(nc.vector.tensor_scalar(turns, turns, -12582912.0, None, ALU.add))
                for part in two_pi_parts():
                    step(nc.vector.scalar_tensor_tensor(angle, turns, -part, angle, ALU.mult, ALU.add))
                nc.vector.tensor_scalar(r, angle, 3.1415925, -3.1415925, ALU.min, ALU.max).then_inc(angles, 1)
                dve.wait_ge(angles, 2 * layer + 1)
                step(nc.vector.scalar_tensor_tensor(turns, r, -1.0, r, ALU.mult, ALU.max))
                nc.vector.tensor_scalar(sq[:, 3, :], turns, -1.0, math.pi / 2, ALU.mult, ALU.add).then_inc(angles, 1)
                dve.wait_ge(tables, 2 * layer + 2)

            def attention(a, take, probs, head_out=None):
                mids = 0

                def mid(ins):
                    nonlocal mids
                    mids += 1
                    ins.then_inc(a.mid, 1)
                    dve.wait_ge(a.mid, mids)

                for t in range(a.n + 2):
                    if t < a.n:
                        dve.wait_ge(a.scores, t + 1)
                        take(a, t, mid)
                    if 1 <= t <= a.n:
                        probs(a, t - 1, mid)
                    if head_out and t > a.steps and (t - 1) % a.steps == 0:
                        head_out((t - 1) // a.steps - 1)

            def take_max(width, count, scale):
                def take(a, t, mid):
                    b = 2 * (t % 2)
                    mid(nc.vector.tensor_reduce(small[:, t % 2, 0:count], ps[:, b:b + count, 0:width], AX.X, ALU.max))
                    nc.vector.tensor_scalar(small[:, t % 2, 2:2 + count], small[:, t % 2, 0:count], -scale, None,
                                            ALU.mult).then_inc(a.taken, 1)
                return take

            def take_masked(a, t, mid):
                if t >= 2:
                    dve.wait_ge(a.turned, t - 1)
                w, b = a.blocks * P, 2 * (t % 2)
                mid(nc.vector.tensor_tensor_reduce(
                    out=e_sb[:, t % 2, 0:w], in0=ps[:, b:b + 2, :].rearrange("p b c -> p (b c)")[:, 0:w],
                    in1=mask[:, t % DIL, :], scale=DB_DH ** -0.5, scalar=-3.0e38, op0=ALU.add, op1=ALU.max,
                    accum_out=small[:, t % 2, 0:1]))
                nc.vector.tensor_scalar(small[:, t % 2, 2:3], small[:, t % 2, 0:1], -1.0, None,
                                        ALU.mult).then_inc(a.taken, 1)

            def probs_plain(a, t, mid):
                dve.wait_ge(a.exps, t + 1)
                mid(nc.vector.reciprocal(small[:, t % 2, 6:7], small[:, t % 2, 4:5]))
                e = e_sb[:, t % 2, 0:a.blocks * P]
                nc.vector.tensor_scalar(e, e, small[:, t % 2, 6:7], None, ALU.mult).then_inc(a.probs, 1)

            def probs_diff(a, t, mid):
                s = small[:, t % 2]
                e = e_sb[:, t % 2]
                dve.wait_ge(a.exps, 2 * t + 2)
                mid(nc.vector.reciprocal(s[:, 6:8], s[:, 4:6]))
                mid(nc.vector.tensor_scalar(s[:, 7:8], s[:, 7:8], lam_w[:, 5:6], None, ALU.mult))
                mid(nc.vector.tensor_scalar(e[:, S:2 * S], e[:, S:2 * S], s[:, 7:8], None, ALU.mult))
                nc.vector.scalar_tensor_tensor(e[:, 0:S], e[:, 0:S], s[:, 6:7], e[:, S:2 * S], ALU.mult,
                                               ALU.add).then_inc(a.probs, 1)

            dve.wait_ge(small_loaded, 80)
            nc.vector.tensor_copy(posf[:, :], half[:, 0, :].bitcast(i32)).then_inc(dve_step, 1)
            steps += 1
            nc.vector.tensor_scalar(subg[:, 1:2], subg[:, 0:1], 1.0 - LAMBDA_INIT, None, ALU.mult)
            step(nc.vector.tensor_tensor(lam_sb[:, 0, :], lam_sb[:, 0, :], lam_sb[:, 1, :], ALU.mult))
            step(nc.vector.tensor_tensor(lam_sb[:, 2, :], lam_sb[:, 2, :], lam_sb[:, 3, :], ALU.mult))
            for n in range(2):
                nc.vector.tensor_reduce(lam_w[:, n:n + 1], lam_sb[:, 2 * n, :], AX.X, ALU.add).then_inc(lam_sums, 1)
            dve.wait_ge(constants, 4)
            step(nc.vector.tensor_reduce(phase4[:, :], ident[:, :].rearrange("p (a b) -> p b a", b=DIL), AX.X, ALU.add))
            nc.vector.tensor_scalar(phase4[:, :], phase4[:, :], -MASKED, MASKED, ALU.mult,
                                    ALU.add).then_inc(phase_ready, 1)
            rests_of(0)
            rests_of(1)
            normalise("pre0", x_sb, 0, "mix_pre_g", act_hi, act_lo)
            reduced_angles(0)
            dve.wait_ge(lam_exp, 1)
            step(nc.vector.tensor_tensor(lam_w[:, 4:5], lam_w[:, 3:4], lam_w[:, 2:3], ALU.subtract))
            step(nc.vector.tensor_scalar(lam_w[:, 5:6], lam_w[:, 4:5], -LAMBDA_INIT, None, ALU.add))
            u = UNITS["qkv0"]
            for n in range(4):
                dst = q0 if n < 2 else k0
                rope_banks(u + n, lambda m, dst=dst, n=n: dst[:, 4 * (n % 2) + m:4 * (n % 2) + m + 1, :],
                           4 * n, DA_DQ // 2)
            for n in range(2):
                unit(u + 4 + n)
            attention(att_d, take_max(S, 2, DA_DQ ** -0.5), probs_diff)
            for h in range(DA_HEADS + 1):
                if h < DA_HEADS:
                    dve.wait_ge(sub_rstd, h + 1)
                    stage_free("o0", h)
                    nc.vector.scalar_tensor_tensor(stage[:, h % 2, :], y_sb[:, h, :], subg[:, 1:2], half[:, h % 2, :],
                                                   ALU.mult, ALU.mult).then_inc(staged, 1)
                if h >= 1:
                    dve.wait_ge(staged, STAGED["o0"] + h)
                    rest("o0", h - 1, act_lo[:, h - 1, :], act_hi[:, h - 1, :], stage[:, (h - 1) % 2, :])

            for layer in range(2):
                if layer == 1:
                    normalise("pre1", x_sb, 1, "mix_pre_g", act_hi, act_lo)
                    reduced_angles(1)
                    for h in range(2):
                        u = UNITS["qkv1a" if h == 0 else "qkv1b"]
                        with dve.Fori(0, GROUPS) as g:
                            for kind, dst in enumerate((q1, k1)):
                                rope_banks(u + kind, lambda m, dst=dst: dst[:, bass.ds(g, 1), m, :],
                                           16 + 8 * GROUPS * h + 4 * kind, DB_DH // 2, g)
                        for g in range(GROUPS):
                            unit(u + 2 * GROUPS + g)
                        if h == 0:
                            dve.wait_ge(mask_step, MASK_STEPS)
                        attention(att_l[h], take_masked, probs_plain)
                    for k in range(KT):
                        rest("o1", k, act_lo[:, k, :], act_hi[:, k, :], y_sb[:, k, :])

                unit(UNITS[f"o{layer}"])
                normalise(f"mem{layer}", mem_sb, layer, "mem_g", mem_hi, mem_lo, MEM)
                unit(UNITS[f"o{layer}"] + 1)
                u = UNITS[f"kv{layer}"]
                unit(u)
                add_normalised(f"mix{layer}", layer, "mix_post_g", 3 * layer)
                unit(u + 1)
                normalise(f"xpre{layer}", x_sb, layer, "xa_pre_g", act_hi, act_lo)
                unit(u + 2)
                unit(u + 3)
                for n in range(2):
                    unit(UNITS[f"xq{layer}"] + n)

                a = att_x[layer]

                def head_rests(h):
                    for k in range(XB * h, XB * (h + 1)):
                        rest(f"xo{layer}", k, act_lo[:, k, :], act_hi[:, k, :], ps[:, 6 + k % XB, :])

                attention(a, take_max(MEM, 1, XA_DH ** -0.5), probs_plain, head_rests)
                for n in range(2):
                    unit(UNITS[f"xo{layer}"] + n)
                add_normalised(f"xa{layer}", layer, "xa_post_g", 3 * layer + 1)
                normalise(f"fpre{layer}", x_sb, layer, "ffn_pre_g", act_hi, act_lo)

                u, first, split = UNITS[f"ff{layer}"], STAGED[f"ff{layer}"], SPLITS[f"ff{layer}"]
                dve.wait_ge(y_cleared, layer + 1)

                def chunk(c):
                    def square_of(up):
                        def bank(m):
                            n = 4 * up + m
                            dve.wait_ge(bank_out[(u + up) % 2], banks_out(u + up, m, c * 2))
                            dve.wait_ge(hi_ready, c * KT + (split + n - 1))
                            dve.wait_ge(lo_ready, c * KT + (split + n - 1))
                            nc.vector.tensor_tensor(stage[:, n % 2, :], half[:, n % 2, :], half[:, n % 2, :],
                                                    ALU.mult).then_inc(staged, 1)
                            if n >= 1:
                                square_rest(n - 1)
                        return bank

                    def square_rest(n):
                        dve.wait_ge(hi_ready, c * KT + (split + n + 1))
                        dve.wait_ge(staged, c * KT + (first + n + 1))
                        nc.vector.tensor_tensor(ff_lo[:, n, :], stage[:, n % 2, :], ff_hi[:, n, :].bitcast(f32),
                                                ALU.subtract).then_inc(lo_ready, 1)

                    unit(u, square_of(0), c * 2)
                    unit(u + 1, square_of(1), c * 2)
                    square_rest(KT - 1)
                    unit(u + 2, share_of(0, c), c * 2)

                def share_of(down, c, v=None):
                    v = u + 2 + down if v is None else v

                    def bank(m):
                        tile = y_sb[:, 4 * down + m, :]
                        dve.wait_ge(bank_done, c * 16 + (4 * v + m + 1))
                        dve.wait_ge(bank_out[v % 2], banks_out(v - 2, m, c * 2))
                        nc.vector.tensor_tensor(tile, ps[:, 4 * (v % 2) + m, :], tile,
                                                ALU.add).then_inc(bank_out[v % 2], 1)
                    return bank

                with dve.Fori(0, CHUNKS - 1) as c:
                    chunk(c)
                    unit(u + 3, share_of(1, c), c * 2)
                chunk(CHUNKS - 1)
                last = u + 4 * CHUNKS - 1
                unit(last, share_of(1, 0, last))
                add_normalised(f"ff{layer}", layer, "ffn_post_g", 3 * layer + 2)

        @block.tensor
        def _(pe):
            def unit(u, hi, lo, split, ii=0, split_ii=0, tokens=None, nb=4, width=NB, stat=None):
                s = 4 * (u % 2)
                if u >= 2:
                    pe.wait_ge(bank_out[u % 2], ii * 4 + 4 * (u // 2))
                for j in range(4):
                    pe.wait_ge(w_lo_ready, ii * 8 + (4 * u + j + 1))
                    for a in range(2):
                        k = 2 * j + a
                        pe.wait_ge(lo_ready, split_ii * KT + (split + k + 1))
                        for m in range(nb):
                            if stat and k == 0 and m == 3:
                                pe.wait_ge(ln_done, STATS[stat] + 1)
                            wh, wl = w_hi[:, j % 2, a], w_lo[:, j % 2, a]
                            if tokens is None:
                                c = slice(m * P, (m + 1) * P)
                                passes = ((wl[:, c], hi[:, k]), (wh[:, c], lo[:, k]), (wh[:, c], hi[:, k]))
                            else:
                                th, tl = tokens(hi[:, k], m), tokens(lo[:, k], m)
                                passes = ((tl, wh), (th, wl), (th, wh))
                            for n, (left, right) in enumerate(passes):
                                last = nc.tensor.matmul(ps[:, s + m, 0:width], left, right,
                                                        start=(k == 0 and n == 0), stop=(k == KT - 1 and n == 2))
                            if k == KT - 1:
                                last.then_inc(bank_done, 4 // nb)
                    if j < 3:
                        last.then_inc(pair_used, 1)

            def natural(ap, m):
                return ap[:, m * P:(m + 1) * P]

            def statistic(name, width=S):
                n = STATS[name]
                if STAT_BEFORE[name] >= 2:
                    v = STAT_BEFORE[name]
                    pe.wait_ge(bank_out[v % 2], 4 * (v // 2))
                for k in range(KT):
                    pe.wait_ge(sq_ready, KT * n + k + 1)
                    last = nc.tensor.matmul(ps[:, stat_bank(name), 0:width], ones[:, :], sq[:, k, 0:width],
                                            start=(k == 0), stop=(k == KT - 1))
                last.then_inc(stat_done, 1)

            def attention(a, scores, scores_read, per_step, weigh, o_free):
                for t in range(a.n + 2):
                    if t < a.n:
                        if t >= 2:
                            pe.wait_ge(scores_read, per_step * (t - 1))
                        scores(t // a.steps, t % a.steps, t).then_inc(a.scores, 1)
                    if 1 <= t <= a.n:
                        n = t - 1
                        pe.wait_ge(a.probs, n + 1)
                        copied = n if a.wide else n - 1
                        if copied > 0:
                            pe.wait_ge(a.pT, copied)
                        for b in range(a.blocks):
                            last = nc.tensor.transpose(a.turn_banks(n, b), e_sb[:, n % 2, b * P:(b + 1) * P],
                                                       ident[:, :])
                        last.then_inc(a.turned, 1)
                    if t >= 2:
                        n = t - 2
                        pe.wait_ge(a.pT, n + 1)
                        if n % a.steps == 0:
                            o_free(n // a.steps)
                        weigh(n // a.steps, n % a.steps, n).then_inc(a.weighed, 1)

            def o_read(a):
                def o_free(h):
                    if h >= 2:
                        pe.wait_ge(a.o_out, h - 1)
                return o_free

            def p_of(n, b):
                return pT_sb[:, n % 2, b * P:(b + 1) * P]

            pe.wait_ge(constants, 4)
            statistic("pre0")
            u = UNITS["qkv0"]
            for n in range(4):
                unit(u + n, act_hi, act_lo, SPLITS["pre0"], stat="pre0" if n == 0 else None)
            for n in range(2):
                unit(u + 4 + n, act_hi, act_lo, SPLITS["pre0"], tokens=natural)

            pe.wait_ge(rope_done, 16)
            for n in range(2):
                pe.wait_ge(bank_out[(u + 4 + n) % 2], banks_out(u + 4 + n, 3))

            def scores_diff(h, s, t):
                for c in range(2):
                    r = slice(c * DA_DQ, (c + 1) * DA_DQ)
                    last = nc.tensor.matmul(ps[:, 2 * (t % 2) + c, :], q0[r, h, s * P:(s + 1) * P], k0[r, h, :],
                                            start=True, stop=True)
                return last

            def weigh_diff(h, s, n):
                for b in range(S // P):
                    last = nc.tensor.matmul(ps[:, 6 + h % 2, s * P:(s + 1) * P], v0[:, b, h * P:(h + 1) * P],
                                            p_of(n, b), start=(b == 0), stop=(b == S // P - 1))
                return last

            attention(att_d, scores_diff, att_d.exps, 2, weigh_diff, o_read(att_d))
            pe.wait_ge(att_d.o_out, DA_HEADS)
            for h in range(DA_HEADS):
                pe.wait_ge(sub_sq, h + 1)
                if h >= 4:
                    pe.wait_ge(sub_ln, h - 3)
                nc.tensor.matmul(ps[:, 4 + h % 4, :], ones[:, :], sq[:, h, :], start=True,
                                 stop=True).then_inc(sub_stat, 1)

            for layer in range(2):
                if layer == 1:
                    statistic("pre1")
                    for h in range(2):
                        u = UNITS["qkv1a" if h == 0 else "qkv1b"]
                        if h == 0:
                            pe.wait_ge(ln_done, STATS["pre1"] + 1)
                        with pe.Fori(0, GROUPS) as g:
                            for kind in range(2):
                                unit(u + kind, act_hi, act_lo, SPLITS["pre1"], g)
                        for g in range(GROUPS):
                            unit(u + 2 * GROUPS + g, act_hi, act_lo, SPLITS["pre1"],
                                 tokens=natural if g == 0 else residue)
                        pe.wait_ge(rope_done, 16 + 8 * GROUPS * (h + 1))
                        for g in range(GROUPS):
                            v = u + 2 * GROUPS + g
                            pe.wait_ge(bank_out[v % 2], banks_out(v, 3))

                        def scores_dilated(h, r, t):
                            b = 2 * (t % 2)
                            nc.tensor.matmul(ps[:, b, :], residue(q1[:, 0, h, :], r), k1[:, 0, h, :],
                                             start=True, stop=True)
                            for g in (1, 2):
                                last = nc.tensor.matmul(ps[:, b + 1, (g - 1) * P:g * P], residue(q1[:, g, h, :], r),
                                                        residue(k1[:, g, h, :], r), start=True, stop=True)
                            return last

                        def weigh_dilated(h, r, n):
                            for b in range(S // P + 2):
                                g, tile = (0, b) if b < S // P else (b - S // P + 1, r)
                                last = nc.tensor.matmul(ps[:, 6 + h % 2, r * P:(r + 1) * P],
                                                        v1[:, g, tile, h * P:(h + 1) * P], p_of(n, b),
                                                        start=(b == 0), stop=(b == S // P + 1))
                            return last

                        attention(att_l[h], scores_dilated, att_l[h].taken, 1, weigh_dilated, o_read(att_l[h]))
                        pe.wait_ge(att_l[h].o_out, HALF)

                o = UNITS[f"o{layer}"]
                split = SPLITS[f"o{layer}"]
                unit(o, act_hi, act_lo, split)
                statistic(f"mem{layer}", MEM)
                if layer == 0:
                    pe.wait_ge(sub_ln, DA_HEADS)
                unit(o + 1, act_hi, act_lo, split, stat=f"mem{layer}")
                u = UNITS[f"kv{layer}"]
                split = SPLITS[f"mem{layer}"]
                unit(u, mem_hi, mem_lo, split, tokens=natural, nb=2)
                statistic(f"mix{layer}")
                unit(u + 1, mem_hi, mem_lo, split, tokens=natural, nb=2)
                statistic(f"xpre{layer}")
                unit(u + 2, mem_hi, mem_lo, split, width=MEM, stat=f"xpre{layer}")
                unit(u + 3, mem_hi, mem_lo, split, width=MEM)
                u = UNITS[f"xq{layer}"]
                for n in range(2):
                    unit(u + n, act_hi, act_lo, SPLITS[f"xpre{layer}"])

                for v in [UNITS[f"kv{layer}"] + n for n in range(4)] + [u, u + 1]:
                    pe.wait_ge(bank_out[v % 2], banks_out(v, 3))

                def scores_cross(h, s, t):
                    for b in range(XB):
                        last = nc.tensor.matmul(ps[:, 2 * (t % 2), 0:MEM], xq[:, XB * h + b, s * P:(s + 1) * P],
                                                xk[:, XB * h + b, :], start=(b == 0), stop=(b == XB - 1))
                    return last

                def weigh_cross(h, s, n):
                    for d in range(XB):
                        for b in range(MEM // P):
                            c = (XB * h + d) * P
                            last = nc.tensor.matmul(ps[:, 6 + d, s * P:(s + 1) * P], xv[:, b, c:c + P], p_of(n, b),
                                                    start=(b == 0), stop=(b == MEM // P - 1))
                    return last

                def split_read(h):
                    if h >= 1:
                        pe.wait_ge(lo_ready, SPLITS[f"xo{layer}"] + XB * h)

                a = att_x[layer]
                attention(a, scores_cross, a.exps, 1, weigh_cross, split_read)
                for n in range(2):
                    unit(UNITS[f"xo{layer}"] + n, act_hi, act_lo, SPLITS[f"xo{layer}"])
                statistic(f"xa{layer}")
                pe.wait_ge(ln_done, STATS[f"xa{layer}"] + 1)
                statistic(f"fpre{layer}")
                pe.wait_ge(ln_done, STATS[f"fpre{layer}"] + 1)

                u = UNITS[f"ff{layer}"]
                with pe.Fori(0, CHUNKS) as c:
                    for n in range(2):
                        unit(u + n, act_hi, act_lo, SPLITS[f"fpre{layer}"], c * 2)
                    for n in range(2):
                        unit(u + 2 + n, ff_hi, ff_lo, SPLITS[f"ff{layer}"], c * 2, split_ii=c)
                statistic(f"ff{layer}")
                pe.wait_ge(ln_done, STATS[f"ff{layer}"] + 1)


MASK_STEPS = 1 + DIL * 6


def kernel(**inputs):
    import concourse.bacc as _bacc
    from concourse.bass_utils import run_bass_kernel_spmd as _run

    def lay(a, features=True):
        return np.ascontiguousarray(a.T.reshape(-1, P, a.shape[0]).transpose(1, 0, 2))

    a = {name: np.asarray(value) for name, value in inputs.items()}
    gains = np.stack([a[name][layer] for layer in range(2) for name in LAYER_GAINS])
    arrays = {
        "x": lay(a["x"][0]),
        "mem": lay(a["mem"][0]),
        "positions": np.ascontiguousarray(a["positions"]),
        "gains": np.ascontiguousarray(gains.reshape(len(gains), KT, P).transpose(2, 0, 1)),
        "consts": rope_columns(),
        "lam": np.ascontiguousarray(a["da_lambda"].reshape(1, -1)),
        "subln_g": np.ascontiguousarray(a["da_subln_g"].reshape(P, 1)),
        "da_w_qkv": a["da_w_qkv"][0], "da_w_o": a["da_w_o"][0],
        "db_w_qkv": a["db_w_qkv"][0], "db_w_o": a["db_w_o"][0],
        "xa_wq": a["xa_wq"], "xa_wkv": a["xa_wkv"], "xa_wo": a["xa_wo"],
        "w_up": a["w_up"], "w_down": a["w_down"],
    }
    nc = _bacc.Bacc("TRN2", target_bir_lowering=False, num_devices=1)
    aps = {}
    for name, value in arrays.items():
        aps[name] = nc.dram_tensor(f"in_{name}", value.shape, mybir.dt.from_np(value.dtype), kind="ExternalInput").ap()
    out = nc.dram_tensor("out_0", (P, KT, S), mybir.dt.float32, kind="ExternalOutput").ap()
    build(nc, out=out, **aps)
    r = _run(nc, [{f"in_{name}": value for name, value in arrays.items()}], core_ids=[0])
    y = r.results[0]["out_0"]
    return np.ascontiguousarray(y.transpose(2, 1, 0).reshape(1, S, D))
```

```python
import math
from contextlib import ExitStack

import numpy as np

import concourse.bass as bass
from concourse import mybir

D = 1024
S = 512
MEM = 256
P = 128
KT = D // P
NB = 512
EPS = 1e-6
THETA = 10000.0
DA_HEADS, DA_DQ = 8, 64
LAMBDA_INIT = 0.8 - 0.6 * math.exp(-0.3 * 0)
GROUPS, DB_DH = 3, 128
HALF = 4
DIL = 4
RADIUS = 64
XA_HEADS, XA_DH = 4, 256
XB = XA_DH // P
FF = 4 * D
CHUNKS = FF // D
MASKED = -1.0e37
LAYER_GAINS = ["mix_pre_g", "mix_post_g", "xa_pre_g", "mem_g", "xa_post_g", "ffn_pre_g", "ffn_post_g"]

C_INV0, C_SIGN0, C_INV1, C_SIGN1 = range(4)


def rope_columns():
    cols = np.zeros((P, 4), np.float32)
    for at, dh in ((0, DA_DQ), (2, DB_DH)):
        inv = np.float32(THETA) ** (-np.arange(0, dh, 2, dtype=np.float32) / np.float32(dh))
        row = np.arange(P) % dh
        cols[:, at] = inv.astype(np.float32)[row % (dh // 2)]
        cols[:, at + 1] = np.where(row < dh // 2, 1.0, -1.0)
    return cols


def two_pi_parts():
    parts, rest = [], 2 * math.pi
    for bits in (8, 9, 9):
        e = math.floor(math.log2(rest)) - bits + 1
        part = math.floor(rest / 2.0**e) * 2.0**e
        parts.append(part)
        rest -= part
    return parts + [rest]


def numbered(names, sizes):
    at, n = {}, 0
    for name, size in zip(names, sizes):
        at[name] = n
        n += size
    return at, n


UNITS, TOTAL_UNITS = numbered(
    ["qkv0", "o0", "kv0", "xq0", "xo0", "ff0", "qkv1a", "qkv1b", "o1", "kv1", "xq1", "xo1", "ff1"],
    [6, 2, 4, 2, 2, 4 * CHUNKS, 3 * GROUPS, 3 * GROUPS, 2, 4, 2, 2, 4 * CHUNKS])
SPLIT_NAMES = ["pre0", "o0", "mem0", "xpre0", "xo0", "fpre0", "ff0", "pre1", "o1", "mem1", "xpre1", "xo1",
               "fpre1", "ff1"]
SPLITS, _ = numbered(SPLIT_NAMES, [KT * CHUNKS if n.startswith("ff") else KT for n in SPLIT_NAMES])
STAGED_NAMES = [n for n in SPLIT_NAMES if n not in ("o0", "xo0", "o1", "xo1")]
STAGED, _ = numbered(STAGED_NAMES, [KT * CHUNKS if n.startswith("ff") else KT for n in STAGED_NAMES])
STAT_NAMES = ["pre0", "mem0", "mix0", "xpre0", "xa0", "fpre0", "ff0",
              "pre1", "mem1", "mix1", "xpre1", "xa1", "fpre1", "ff1"]
STATS, _ = numbered(STAT_NAMES, [1] * len(STAT_NAMES))
STAT_BEFORE = {"pre0": UNITS["qkv0"] + 1, "ff0": UNITS["qkv1a"], "pre1": UNITS["qkv1a"] + 1, "ff1": TOTAL_UNITS}
for _l in "01":
    STAT_BEFORE.update({"mem" + _l: UNITS["o" + _l] + 1, "mix" + _l: UNITS["kv" + _l], "xpre" + _l: UNITS["xq" + _l],
                        "xa" + _l: UNITS["ff" + _l], "fpre" + _l: UNITS["ff" + _l] + 1})


POOLED = {n: 4 if n[:2] in ("mi", "xa", "ff") else KT for n in STAT_NAMES}


def summed(name, k=None):
    before = sum(POOLED[n] - 1 for n in STAT_NAMES[:STATS[name]])
    return before + (POOLED[name] - 1 if k is None else k)


def stat_bank(name):
    return 4 * (STAT_BEFORE[name] % 2) + 3


def banks_out(u, m, ii=0, nb=4):
    return ii * 4 + (4 * (u // 2) + (m + 1) * (4 // nb))


def residue(ap, r):
    return ap.rearrange("p (l r) -> p r l", r=DIL)[:, r]


def build(nc, x, mem, positions, gains, consts, lam, subln_g, da_w_qkv, da_w_o, db_w_qkv, db_w_o,
          xa_wq, xa_wkv, xa_wo, w_up, w_down, out):
    f32, f32r, bf16, i32 = mybir.dt.float32, mybir.dt.float32r, mybir.dt.bfloat16, mybir.dt.int32
    ACT = mybir.ActivationFunctionType
    ALU = mybir.AluOpType
    AX = mybir.AxisListType

    def tiles(w):
        return w.rearrange("(r a p) (n c) -> r n p a c", a=2, p=P, c=NB)

    with ExitStack() as ctx:
        def sb(name, shape, dt=f32, scope=ctx):
            return scope.enter_context(nc.sbuf_tensor(name, shape, dt))

        def sem(name):
            return ctx.enter_context(nc.semaphore(name))

        x_sb = sb("x_sb", [P, KT, S])
        y_sb = sb("y_sb", [P, KT, S])
        act_hi = sb("act_hi", [P, KT, S], f32r)
        act_lo = sb("act_lo", [P, KT, S], f32r)
        raw = sb("raw", [P, 4, 2, NB])
        w_hi = sb("w_hi", [P, 2, 2, NB], f32r)
        w_lo = sb("w_lo", [P, 2, 2, NB], f32r)
        cos_sb = sb("cos_sb", [P, 1, S])
        sin_sb = sb("sin_sb", [P, 1, S])
        posf = sb("posf", [P, S])
        mask = sb("mask", [P, DIL, S + 2 * P], bf16)
        stage = sb("stage", [P, 2, S])
        half = sb("half", [P, 2, S])
        rstd = sb("rstd", [P, S])
        gain = sb("gain", [P, 2 * len(LAYER_GAINS), KT])
        cst = sb("cst", [P, 4])
        lam_sb = half[:, 1, 0:4 * DA_DQ].rearrange("p (a b) -> p a b", a=4)
        lam_w = sb("lam_w", [P, 8])
        subg = sb("subg", [P, 2])
        ones = sb("ones", [P, P])
        ident = sb("ident", [P, P])
        phase4 = sb("phase4", [P, DIL])
        eps = sb("eps", [P, 1])
        rstd_cols = sb("rstd_cols", [P, 2 * DIL])
        small = sb("small", [P, 2, 8])
        with ExitStack() as scope:
            e_sb = sb("e_sb", [P, 3, 1024], scope=scope)
            pT_sb = sb("pT_sb", [P, 2, S], scope=scope)
        with ExitStack() as scope:
            el_sb = sb("el_sb", [P, 3, S + 2 * P], scope=scope)
            plT_sb = sb("plT_sb", [P, 2, S + 2 * P], scope=scope)
        with ExitStack() as scope:
            ex_sb = sb("ex_sb", [P, 4, MEM], scope=scope)
            pxT_sb = sb("pxT_sb", [P, 2, MEM], scope=scope)
        sq = sb("sq", [P, KT, S])
        with ExitStack() as scope:
            q0 = sb("q0", [P, DA_HEADS, S], scope=scope)
            k0 = sb("k0", [P, DA_HEADS, S], scope=scope)
            v0 = sb("v0", [P, S // P, D], scope=scope)
        with ExitStack() as scope:
            q1 = sb("q1", [P, GROUPS, HALF, S], scope=scope)
            k1 = sb("k1", [P, GROUPS, HALF, S], scope=scope)
            v1 = sb("v1", [P, GROUPS, S // P, HALF * P], scope=scope)
        with ExitStack() as scope:
            xq = sb("xq", [P, KT, S], scope=scope)
            xk = sb("xk", [P, KT, MEM], scope=scope)
            xv = sb("xv", [P, MEM // P, D], scope=scope)
            mem_sb = sb("mem_sb", [P, KT, MEM], scope=scope)
            mem_hi = sb("mem_hi", [P, KT, MEM], f32r, scope=scope)
            mem_lo = sb("mem_lo", [P, KT, MEM], f32r, scope=scope)
            mem_sq = sb("mem_sq", [P, KT, MEM], scope=scope)
        with ExitStack() as scope:
            ff_hi = sb("ff_hi", [P, KT, S], f32r, scope=scope)
            ff_lo = sb("ff_lo", [P, KT, S], f32r, scope=scope)
        ps = ctx.enter_context(nc.psum_tensor("ps", [P, 8, NB], f32))

        raw_loaded = [sem(f"raw_loaded{j}") for j in range(4)]
        w_hi_ready = sem("w_hi_ready")
        w_lo_ready = sem("w_lo_ready")
        pair_used = sem("pair_used")
        bank_done = sem("bank_done")
        bank_out = [sem("bank_out0"), sem("bank_out1")]
        hi_ready = sem("hi_ready")
        lo_ready = sem("lo_ready")
        staged = sem("staged")
        sq_ready = sem("sq_ready")
        sq_summed = sem("sq_summed")
        stat_done = sem("stat_done")
        ln_done = sem("ln_done")
        rstd_ready = sem("rstd_ready")
        y_scaled = sem("y_scaled")
        x_ready = sem("x_ready")
        y_cleared = sem("y_cleared")
        rope_done = sem("rope_done")
        sub_sq = sem("sub_sq")
        sub_stat = sem("sub_stat")
        sub_ln = sem("sub_ln")
        sub_rstd = sem("sub_rstd")
        sub_y = sem("sub_y")
        cols_done = sem("cols_done")
        cols_read = sem("cols_read")
        tables_scaled = sem("tables_scaled")
        x_loaded = [sem(f"x_loaded{j}") for j in range(KT // 2)]
        gain_loaded = sem("gain_loaded")
        small_loaded = sem("small_loaded")
        mem_loaded = sem("mem_loaded")
        dve_step = sem("dve_step")
        constants = sem("constants")
        phase_ready = sem("phase_ready")
        mask_step = sem("mask_step")
        angles = sem("angles")
        tables = sem("tables")
        lam_sums = sem("lam_sums")
        lam_exp = sem("lam_exp")
        out_done = sem("out_done")

        class Attention:

            def __init__(self, name, heads, blocks, wide=False, narrow=False):
                self.heads, self.steps, self.blocks = heads, S // P, blocks
                self.wide = wide
                self.single = wide or blocks == S // P
                self.depth = 4 if narrow else 2
                self.lag = 3 if narrow else 2
                self.n = heads * self.steps
                self.e, self.p = (el_sb, plT_sb) if wide else (ex_sb, pxT_sb) if narrow else (e_sb, pT_sb)
                self.scores = sem(name + "_scores")
                self.taken = sem(name + "_taken")
                self.exps = sem(name + "_exps")
                self.probs = sem(name + "_probs")
                self.mid = sem(name + "_mid")
                self.turned = sem(name + "_turned")
                self.pT = sem(name + "_pT")
                self.weighed = sem(name + "_weighed")
                self.o_out = sem(name + "_o_out")

            def turn_banks(self, n, b):
                if self.wide:
                    return ps[:, 4 + b // 4, (b % 4) * P:(b % 4 + 1) * P]
                return ps[:, 4 if self.single else 4 + n % 2, b * P:(b + 1) * P]

            def turned_all(self, n):
                if self.wide:
                    return ps[:, 4:6, :].rearrange("p b c -> p (b c)")[:, 0:self.blocks * P]
                return ps[:, 4 if self.single else 4 + n % 2, 0:self.blocks * P]

            def score_bank(self, t):
                return t % 4 if self.depth == 4 else 2 * (t % 2)

        att_d = Attention("diff", DA_HEADS, S // P)
        att_l = [Attention(f"dil{h}", HALF, S // P + 2, wide=True) for h in range(2)]
        att_x = [Attention(f"cross{i}", XA_HEADS, MEM // P, narrow=True) for i in range(2)]

        def gcol(layer, name, k):
            n = layer * len(LAYER_GAINS) + LAYER_GAINS.index(name)
            return gain[:, n, k:k + 1]

        block = ctx.enter_context(nc.Block())

        @block.sync
        def _(sp):
            def load_unit(u, w, row_pair, col, ii=0):
                for j in range(4):
                    if u > 0:
                        sp.wait_ge(w_lo_ready, ii * 8 + (4 * u + j - 3))
                    src = w[bass.ds(row_pair + j, 1), bass.ds(col, 1)]
                    sp.dma_start(raw[:, j], src[0, 0]).then_inc(raw_loaded[j], 16)

            sp.dma_start(gain[:, :, :], gains).then_inc(gain_loaded, 16)
            for k in range(0, KT, 2):
                sp.dma_start(x_sb[:, k:k + 2, :], x[:, k:k + 2]).then_inc(x_loaded[k // 2], 16)
                if k == 0:
                    w = tiles(da_w_qkv)
                    load_unit(0, w, 0, 0)
            sp.dma_start(cst[:, :], consts).then_inc(small_loaded, 16)
            sp.dma_start(half[:, 0, :].bitcast(i32), positions.broadcast_to([P, S])).then_inc(small_loaded, 16)
            sp.dma_start(half[:, 1, 0:4 * DA_DQ],
                         lam.broadcast_to([P, 4 * DA_DQ])).then_inc(small_loaded, 16)
            sp.dma_start(subg[:, 0:1], subln_g).then_inc(small_loaded, 16)
            for n in range(1, 6):
                load_unit(n, w, 0, n)

            def after_attention(layer, att):
                u = UNITS[f"o{layer}"]
                w = tiles(da_w_o if layer == 0 else db_w_o)
                load_unit(u, w, 0, 0)
                sp.wait_ge(att.weighed, att.n)
                sp.dma_start(mem_sb[:, :, :], mem).then_inc(mem_loaded, 16)
                load_unit(u + 1, w, 0, 1)
                w = tiles(xa_wkv[layer])
                for n, col in enumerate((2, 3, 0, 1)):
                    load_unit(UNITS[f"kv{layer}"] + n, w, 0, col)
                for name, w in (("xq", xa_wq), ("xo", xa_wo)):
                    for n in range(2):
                        load_unit(UNITS[f"{name}{layer}"] + n, tiles(w[layer]), 0, n)
                u = UNITS[f"ff{layer}"]
                up, down = tiles(w_up[layer]), tiles(w_down[layer])
                load_unit(u, up, 0, 0)
                with sp.Fori(0, CHUNKS - 1) as c:
                    load_unit(u + 1, up, 0, c * 2 + 1, c * 2)
                    for n in range(2):
                        load_unit(u + 2 + n, down, c * 4, n, c * 2)
                    load_unit(u + 4, up, 0, c * 2 + 2, c * 2)
                u += 4 * (CHUNKS - 1)
                load_unit(u + 1, up, 0, 2 * CHUNKS - 1)
                for n in range(2):
                    load_unit(u + 2 + n, down, 4 * (CHUNKS - 1), n)

            after_attention(0, att_d)
            w = tiles(db_w_qkv)
            for h in range(2):
                u = UNITS["qkv1a" if h == 0 else "qkv1b"]
                load_unit(u, w, 0, h)
                with sp.Fori(0, GROUPS - 1) as g:
                    load_unit(u + 1, w, 0, g * 2 + (2 * GROUPS + h), g)
                    load_unit(u + 2, w, 0, g * 2 + (2 + h), g)
                load_unit(u + 2 * GROUPS - 1, w, 0, 4 * GROUPS - 2 + h)
                for g in range(GROUPS):
                    load_unit(u + 2 * GROUPS + g, w, 0, 4 * GROUPS + 2 * g + h)
            after_attention(1, att_l[1])
            for k in range(KT):
                sp.wait_ge(x_ready, 5 * KT + k + 1)
                sp.dma_start(out[:, k], x_sb[:, k, :]).then_inc(out_done, 16)
            sp.wait_ge(out_done, 16 * KT)

        @block.gpsimd
        def _(pool):
            sums = 0

            def square_sum(name, k, squares):
                nonlocal sums
                if k == 0:
                    return
                pool.wait_ge(sq_ready, KT * STATS[name] + k + 1)
                pool.wait_ge(sq_summed, sums)
                nc.gpsimd.tensor_tensor(squares[:, 0, :], squares[:, 0, :], squares[:, k, :],
                                        ALU.add).then_inc(sq_summed, 1)
                sums += 1
                assert sums == summed(name, k)

            nc.gpsimd.memset(ones[:, :], 1.0).then_inc(constants, 1)
            nc.gpsimd.memset(eps[:, :], EPS).then_inc(constants, 1)
            nc.gpsimd.memset(ident[:, :], 0.0).then_inc(constants, 1)
            pool.wait_ge(constants, 3)
            nc.gpsimd.affine_select(out=ident[:, :], in_=ident[:, :], compare_op=ALU.not_equal, fill=1.0,
                                    base=0, pattern=[[-1, P]], channel_multiplier=1).then_inc(constants, 1)

            for k in range(KT):
                square_sum("pre0", k, sq)

            nc.gpsimd.memset(mask[:, :, 0:S + P], 0.0).then_inc(mask_step, 1)
            steps = 1
            for r in range(DIL):
                for at, width, step, base in ((0, S, DIL, r), (S, P, 1, 0)):
                    part = mask[:, r, at:at + width]
                    for sign in (1, -1):
                        pool.wait_ge(mask_step, steps)
                        nc.gpsimd.affine_select(out=part, in_=part, compare_op=ALU.is_ge, fill=MASKED,
                                                base=RADIUS - sign * base, pattern=[[sign, width]],
                                                channel_multiplier=-sign * step).then_inc(mask_step, 1)
                        steps += 1
                if r == 0:
                    pool.wait_ge(phase_ready, 1)
                for a in range(2):
                    far = mask[:, r, S + P + a * 64:S + P + (a + 1) * 64].rearrange("p (a b) -> p a b", b=DIL)
                    nc.gpsimd.tensor_copy(far, phase4[:, :].rearrange("p (o b) -> p o b", o=1)
                                          .broadcast_to([P, 16, DIL])).then_inc(mask_step, 1)
                    steps += 1
            assert steps == MASK_STEPS

            def rope_sum(value, parity, dst, n):
                pool.wait_ge(bank_out[parity], value)
                nc.gpsimd.tensor_tensor(dst, dst, half[:, n % 2:n % 2 + 1, :], ALU.add).then_inc(rope_done, 1)

            for n in range(16):
                u = UNITS["qkv0"] + n // 4
                dst = (q0 if n < 8 else k0)[:, n % 8:n % 8 + 1, :]
                rope_sum(banks_out(u, n % 4), u % 2, dst, n)
            def residual_sums(post, name=None):
                for k in range(KT + 2):
                    if k < KT:
                        pool.wait_ge(y_scaled, KT * post + k + 1)
                        nc.gpsimd.tensor_tensor(x_sb[:, k, :], x_sb[:, k, :], y_sb[:, k, :],
                                                ALU.add).then_inc(x_ready, 1)
                    if name and k >= 2:
                        square_sum(name, k - 2, sq)

            for layer in range(2):
                for k in range(KT):
                    square_sum(f"mem{layer}", k, mem_sq)
                for k in range(4):
                    square_sum(f"mix{layer}", k, sq)
                residual_sums(3 * layer, f"xpre{layer}")
                for k in range(4):
                    square_sum(f"xa{layer}", k, sq)
                residual_sums(3 * layer + 1, f"fpre{layer}")
                pool.wait_ge(x_ready, KT * (3 * layer + 2))
                nc.gpsimd.memset(y_sb[:, :, :], 0.0).then_inc(y_cleared, 1)
                for k in range(4):
                    square_sum(f"ff{layer}", k, sq)
                residual_sums(3 * layer + 2, "pre1" if layer == 0 else None)
                if layer == 0:
                    for name in ("qkv1a", "qkv1b"):
                        u = UNITS[name]

                        def rope_sums(kind, g, ii):
                            for m in range(HALF):
                                rope_sum(banks_out(u + kind, m, ii), (u + kind) % 2,
                                         (k1 if kind % 2 else q1)[:, g, m, :], m)

                        rope_sums(0, slice(0, 1), 0)
                        with pool.Fori(0, GROUPS - 1) as g:
                            rope_sums(1, bass.ds(g, 1), g)
                            rope_sums(2, bass.ds(g + 1, 1), g)
                        rope_sums(2 * GROUPS - 1, slice(GROUPS - 1, GROUPS), 0)

        @block.scalar
        def _(act):
            def heads_of(g, ii=0):
                act.wait_ge(raw_loaded[g % 4], ii * 32 + 16 * (g // 4 + 1))
                if g >= 2:
                    v, j = divmod(g - 2, 4)
                    if j < 3:
                        act.wait_ge(pair_used, ii * 6 + (3 * v + j + 1))
                    else:
                        act.wait_ge(bank_done, ii * 8 + 4 * (v + 1))
                nc.scalar.activation(w_hi[:, g % 2], raw[:, g % 4], ACT.Copy).then_inc(w_hi_ready, 1)

            def unit(u, bank=None, ii=0, nb=4, between=None):
                for m in range(4):
                    if m < 2:
                        heads_of(4 * u + 2 + m, ii)
                        if between:
                            between(m)
                for m in range(4):
                    if m % 2 == 0 and u + 1 < TOTAL_UNITS:
                        heads_of(4 * u + 4 + m // 2, ii)
                    if bank and m < nb:
                        bank(m)
                    if between and m % 2 == 1:
                        between(2 + m // 2)

            def copies(u, dst, nb=4, width=NB, scale=None, squares_at=None, between=None):
                def bank(m):
                    src = ps[:, 4 * (u % 2) + m, 0:width]
                    act.wait_ge(bank_done, 4 * u + (m + 1) * (4 // nb))
                    if squares_at is not None:
                        nc.scalar.activation(sq[:, squares_at + m, 0:width], src, ACT.Square).then_inc(sq_ready, 1)
                    nc.scalar.activation(dst(m), src, ACT.Copy, scale=scale(m) if scale else 1.0
                                         ).then_inc(bank_out[u % 2], 4 // nb)
                unit(u, bank, nb=nb, between=between)

            def root(name, width=S):
                n = STATS[name]
                act.wait_ge(stat_done, n + 1)
                nc.scalar.activation(rstd[:, 0:width], ps[:, stat_bank(name), 0:width], ACT.Ln,
                                     bias=eps[:, 0:1], scale=1.0 / D).then_inc(ln_done, 1)
                act.wait_ge(ln_done, n + 1)
                nc.scalar.activation(rstd[:, 0:width], rstd[:, 0:width], ACT.Exp,
                                     scale=-0.5).then_inc(rstd_ready, 1)

            def staged_head(name, k, dst, width=S):
                act.wait_ge(staged, STAGED[name] + k + 1)
                nc.scalar.activation(dst[:, k, :], stage[:, k % 2, 0:width], ACT.Copy).then_inc(hi_ready, 1)

            def renew(name, i, x_new, slack=1):
                if slack <= i < KT + slack:
                    k = i - slack
                    x_new(k)
                    nc.scalar.activation(sq[:, k, :], x_sb[:, k, :], ACT.Square).then_inc(sq_ready, 1)
                    staged_head(name, k, act_hi)

            def post_norm(post):
                return lambda k: act.wait_ge(x_ready, KT * post + k + 1)

            def copy_columns(first_unit, n):
                act.wait_ge(cols_done, n)
                nc.scalar.activation(rstd_cols[:, :], ps[:, 4 * (first_unit % 2) + 3, 0:2 * DIL],
                                     ACT.Copy).then_inc(cols_read, 1)
                act.wait_ge(cols_read, n)

            def sines(layer):
                act.wait_ge(angles, 2 * layer + 1)
                s = C_SIGN1 if layer else C_SIGN0
                nc.scalar.activation(sin_sb[:, 0, :], y_sb[:, 2, :], ACT.Sin, scale=cst[:, s:s + 1]).then_inc(tables, 1)
                act.wait_ge(angles, 2 * layer + 2)
                nc.scalar.activation(cos_sb[:, 0, :], y_sb[:, 3, :], ACT.Sin).then_inc(tables, 1)
                nc.scalar.preload_act_table_set("natural_log_exp_and_others")

            def attention(a, exp, *events):
                for t in range(a.n + max(e[0] for e in events) + 1):
                    if t < a.n:
                        act.wait_ge(a.taken, t + 1)
                        if t > a.lag:
                            act.wait_ge(a.turned, t - a.lag)
                        exp(a, t)
                    if a.lag <= t < a.n + a.lag:
                        n = t - a.lag
                        act.wait_ge(a.turned, n + 1)
                        if n >= 2:
                            act.wait_ge(a.weighed, n - 1)
                        nc.scalar.activation(a.p[:, n % 2, 0:a.blocks * P], a.turned_all(n),
                                             ACT.Copy).then_inc(a.pT, 1)
                    for after, event in events:
                        h, off = divmod(t - after, a.steps)
                        if off == 0 and 1 <= h <= a.heads:
                            event(a, h - 1)

            def exp_diff(a, t):
                for c in range(2):
                    nc.scalar.activation(a.e[:, t % (a.lag + 1), c * S:(c + 1) * S], ps[:, a.score_bank(t) + c, :], ACT.Exp,
                                         bias=small[:, t % 2, 2 + c:3 + c], scale=DA_DQ ** -0.5,
                                         accum_out=small[:, t % 2, 4 + c:5 + c]).then_inc(a.exps, 1)

            def exp_cross(a, t):
                nc.scalar.activation(a.e[:, t % (a.lag + 1), 0:MEM], ps[:, a.score_bank(t), 0:MEM], ACT.Exp,
                                     bias=small[:, t % 2, 2:3], scale=XA_DH ** -0.5,
                                     accum_out=small[:, t % 2, 4:5]).then_inc(a.exps, 1)

            def exp_dilated(a, t):
                w = a.blocks * P
                nc.scalar.activation(a.e[:, t % 3, 0:w], a.e[:, t % 3, 0:w], ACT.Exp,
                                     bias=small[:, t % 2, 2:3],
                                     accum_out=small[:, t % 2, 4:5]).then_inc(a.exps, 1)

            def by_token(ap):
                return ap.rearrange("p (l r) -> p r l", r=DIL)

            def by_column(ap):
                return ap.rearrange("p (r l) -> p r l", r=DIL)

            def dilated_to_y(a, h):
                act.wait_ge(a.weighed, a.steps * (h + 1))
                nc.scalar.activation(by_token(y_sb[:, h, :]), by_column(ps[:, 6 + h % 2, :]),
                                     ACT.Copy).then_inc(a.o_out, 1)

            def dilated_split(a, h):
                act.wait_ge(a.weighed, a.steps * (h + 1))
                nc.scalar.activation(by_token(act_hi[:, HALF + h, :]), by_column(ps[:, 6 + h % 2, :]),
                                     ACT.Copy).then_inc(hi_ready, 1)

            def first_half_split(k):
                def event(a, h):
                    if h == 0:
                        act.wait_ge(att_l[0].o_out, k + 1)
                        nc.scalar.activation(act_hi[:, k, :], y_sb[:, k, :], ACT.Copy).then_inc(hi_ready, 1)
                return event

            def diff_out(a, h):
                act.wait_ge(a.weighed, a.steps * (h + 1))
                if h >= 2:
                    act.wait_ge(sub_stat, h - 1)
                nc.scalar.activation(stage[:, h % 2, :], ps[:, 6 + h % 2, :], ACT.Square).then_inc(sub_sq, 1)
                nc.scalar.activation(y_sb[:, h, :], ps[:, 6 + h % 2, :], ACT.Copy).then_inc(a.o_out, 1)

            def diff_root(a, h):
                act.wait_ge(sub_stat, h + 1)
                if h >= 2:
                    act.wait_ge(sub_y, h - 1)
                nc.scalar.activation(half[:, h % 2, :], ps[:, 5, :], ACT.Ln, bias=eps[:, 0:1],
                                     scale=1.0 / P).then_inc(sub_ln, 1)
                act.wait_ge(sub_ln, h + 1)
                nc.scalar.activation(half[:, h % 2, :], half[:, h % 2, :], ACT.Exp,
                                     scale=-0.5).then_inc(sub_rstd, 1)

            def diff_head(a, h):
                act.wait_ge(sub_y, h + 1)
                nc.scalar.activation(act_hi[:, h, :], y_sb[:, h, :], ACT.Copy).then_inc(hi_ready, 1)

            def head_split(a, h):
                act.wait_ge(a.weighed, a.steps * (h + 1))
                for b in range(XB):
                    nc.scalar.activation(act_hi[:, XB * h + b, :], ps[:, 6 + b, :], ACT.Copy).then_inc(hi_ready, 1)

            nc.scalar.preload_act_table_set("natural_log_exp_and_others")
            heads_of(0)
            heads_of(1)
            for i in range(KT + 2):
                renew("pre0", i, lambda k: act.wait_ge(x_loaded[k // 2], 16))

            def tables_between(layer):
                def between(j):
                    if j == 1:
                        sines(layer)
                    if j == 1 and layer == 0:
                        act.wait_ge(lam_sums, 2)
                        nc.scalar.activation(lam_w[:, 2:4], lam_w[:, 0:2], ACT.Exp).then_inc(lam_exp, 1)
                        act.wait_ge(constants, 4)
                return between

            u = UNITS["qkv0"]
            unit(u, lambda m: root("pre0") if m == 0 else None, between=tables_between(0))
            for n in range(1, 4):
                unit(u + n)
            copy_columns(u + 4, 1)
            for n in range(2):
                copies(u + 4 + n, lambda m, n=n: v0[:, m, n * NB:(n + 1) * NB],
                       scale=lambda m: rstd_cols[:, m:m + 1])
            attention(att_d, exp_diff, (2, diff_out), (5, diff_root), (7, diff_head))

            for layer in range(2):
                if layer == 1:
                    for h in range(2):
                        u = UNITS["qkv1a" if h == 0 else "qkv1b"]
                        unit(u, lambda m: root("pre1") if m == 0 and h == 0 else None,
                             between=tables_between(1) if h == 0 else None)
                        with act.Fori(0, GROUPS - 1) as g:
                            unit(u + 1, ii=g)
                            unit(u + 2, ii=g)
                        unit(u + 2 * GROUPS - 1)
                        u += 2 * GROUPS
                        if h == 0:
                            copy_columns(u, 2)
                        for g in range(GROUPS):
                            copies(u + g, lambda m, g=g: v1[:, g, m, :],
                                   scale=lambda m, g=g: rstd_cols[:, m + (DIL if g else 0):][:, 0:1])
                        if h == 0:
                            attention(att_l[h], exp_dilated, (2, dilated_to_y))
                        else:
                            attention(att_l[h], exp_dilated, (2, dilated_split),
                                      *[(k - 3, first_half_split(k)) for k in range(HALF)])

                u = UNITS[f"o{layer}"]

                def mem_squares(j):
                    if j == 0:
                        act.wait_ge(mem_loaded, 16 * (layer + 1))
                        for k in range(KT):
                            nc.scalar.activation(mem_sq[:, k, :], mem_sb[:, k, :], ACT.Square).then_inc(sq_ready, 1)
                    if j == 3:
                        root(f"mem{layer}", MEM)

                def mem_heads(j):
                    for k in (2 * j, 2 * j + 1):
                        staged_head(f"mem{layer}", k, mem_hi, MEM)

                copies(u, lambda m: y_sb[:, m, :], squares_at=0, between=mem_squares)
                copies(u + 1, lambda m: y_sb[:, 4 + m, :], squares_at=4, between=mem_heads)
                root(f"mix{layer}")
                u = UNITS[f"kv{layer}"]
                for n in range(4):
                    def between(j, n=n):
                        renew(f"xpre{layer}", 4 * n + j, post_norm(3 * layer), 2)
                    if n < 2:
                        copies(u + n, lambda m, n=n: xv[:, m, n * NB:(n + 1) * NB], nb=2, between=between)
                    else:
                        copies(u + n, lambda m, n=n: xk[:, 4 * (n - 2) + m, :], width=MEM, between=between)
                u = UNITS[f"xq{layer}"]
                root(f"xpre{layer}")
                unit(u)
                unit(u + 1)
                attention(att_x[layer], exp_cross, (3, head_split))
                u = UNITS[f"xo{layer}"]
                for n in range(2):
                    copies(u + n, lambda m, n=n: y_sb[:, 4 * n + m, :], squares_at=4 * n)
                root(f"xa{layer}")
                for i in range(KT + 2):
                    renew(f"fpre{layer}", i, post_norm(3 * layer + 1))

                u, first, split = UNITS[f"ff{layer}"], STAGED[f"ff{layer}"], SPLITS[f"ff{layer}"]

                def squares_of(up, c):
                    def bank(m):
                        n = 4 * up + m
                        act.wait_ge(bank_out[(u + up) % 2], banks_out(u + up, m, c * 2))
                        act.wait_ge(hi_ready, c * KT + (split + n - 1))
                        act.wait_ge(lo_ready, c * KT + (split + n - 1))
                        nc.scalar.activation(stage[:, n % 2, :], half[:, n % 2, :], ACT.Square).then_inc(staged, 1)
                        act.wait_ge(staged, c * KT + (first + n + 1))
                        nc.scalar.activation(ff_hi[:, n, :], stage[:, n % 2, :], ACT.Copy).then_inc(hi_ready, 1)
                    return bank

                def first_bank(m):
                    if m == 0:
                        root(f"fpre{layer}")
                    squares_of(0, 0)(m)

                unit(u, first_bank)
                with act.Fori(0, CHUNKS - 1) as c:
                    unit(u + 1, squares_of(1, c), c * 2)
                    unit(u + 2, None, c * 2)
                    unit(u + 3, None, c * 2)
                    unit(u + 4, squares_of(0, c + 1), c * 2)
                v = u + 4 * (CHUNKS - 1)
                unit(v + 1, squares_of(1, CHUNKS - 1))
                unit(v + 2)

                def y_squares(j):
                    for k in (2 * j, 2 * j + 1):
                        act.wait_ge(bank_out[(v + 2 + k // 4) % 2], banks_out(v + 2 + k // 4, k % 4))
                        nc.scalar.activation(sq[:, k, :], y_sb[:, k, :], ACT.Square).then_inc(sq_ready, 1)

                unit(v + 3, between=y_squares)
                root(f"ff{layer}")
                if layer == 0:
                    for i in range(KT + 2):
                        renew("pre1", i, post_norm(2))

        @block.vector
        def _(dve):
            steps = 0

            def step(ins):
                nonlocal steps
                steps += 1
                ins.then_inc(dve_step, 1)
                dve.wait_ge(dve_step, steps)

            def rests_of(g, ii=0):
                dve.wait_ge(w_hi_ready, ii * 8 + (g + 1))
                nc.vector.tensor_tensor(w_lo[:, g % 2], raw[:, g % 4], w_hi[:, g % 2].bitcast(f32),
                                        ALU.subtract).then_inc(w_lo_ready, 1)

            def unit(u, bank=None, ii=0, between=None, done=2, ahead=2):
                for j in range(2):
                    if 2 + j >= done:
                        rests_of(4 * u + 2 + j, ii)
                    if between:
                        between(j)
                for m in range(4):
                    if m % 2 == 0 and u + 1 < TOTAL_UNITS:
                        rests_of(4 * u + 4 + m // 2, ii)
                    if m == 3 and ahead == 3:
                        rests_of(4 * u + 6, ii)
                    if bank:
                        bank(m)
                    if between and m % 2 == 1:
                        between(2 + m // 2)

            def rope_banks(u, dst, n0, swap, ii=0, layer=None, **kw):
                def bank(m):
                    if layer is not None and m == 0:
                        scale_tables(layer)
                    src = ps[:, 4 * (u % 2) + m:4 * (u % 2) + m + 1, :]
                    dve.wait_ge(bank_done, ii * 8 + (4 * u + m + 1))
                    nc.vector.tensor_tensor(dst(m), src, cos_sb[:, :, :], ALU.mult)
                    if n0 + m >= 2:
                        dve.wait_ge(rope_done, ii * 8 + (n0 + m - 1))
                    for at in range(0, P, swap):
                        to = at ^ swap
                        last = nc.vector.tensor_tensor(half[to:to + swap, m % 2:m % 2 + 1, :],
                                                       src[at:at + swap], sin_sb[at:at + swap], ALU.mult)
                    last.then_inc(bank_out[u % 2], 1)
                unit(u, bank, ii, **kw)

            def rest(name, k, dst_lo, hi, source):
                dve.wait_ge(hi_ready, SPLITS[name] + k + 1)
                nc.vector.tensor_tensor(dst_lo, source, hi.bitcast(f32), ALU.subtract).then_inc(lo_ready, 1)

            def stage_free(name, k):
                n = SPLITS[name] + k - 1
                if n > 0:
                    dve.wait_ge(hi_ready, n)
                    dve.wait_ge(lo_ready, n)

            def mem_tile(layer, i):
                name = f"mem{layer}"
                if i < KT:
                    stage_free(name, i)
                    nc.vector.scalar_tensor_tensor(stage[:, i % 2, 0:MEM], mem_sb[:, i, :], gcol(layer, "mem_g", i),
                                                   rstd[:, 0:MEM], ALU.mult, ALU.mult).then_inc(staged, 1)
                if i >= 1:
                    dve.wait_ge(staged, STAGED[name] + i)
                    rest(name, i - 1, mem_lo[:, i - 1, :], mem_hi[:, i - 1, :], stage[:, (i - 1) % 2, 0:MEM])

            def renew(name, layer, gains_name, i, x_new, post_norm=None, slack=1):
                if i < KT and post_norm:
                    g_layer, g_name = post_norm
                    nc.vector.scalar_tensor_tensor(y_sb[:, i, :], y_sb[:, i, :], gcol(g_layer, g_name, i),
                                                   rstd[:, :], ALU.mult, ALU.mult).then_inc(y_scaled, 1)
                if name and slack <= i < KT + slack:
                    k = i - slack
                    x_new(k)
                    stage_free(name, k)
                    nc.vector.tensor_scalar(stage[:, k % 2, :], x_sb[:, k, :], gcol(layer, gains_name, k), None,
                                            ALU.mult).then_inc(staged, 1)
                if name and slack < i <= KT + slack:
                    k = i - slack - 1
                    dve.wait_ge(staged, STAGED[name] + k + 1)
                    rest(name, k, act_lo[:, k, :], act_hi[:, k, :], stage[:, k % 2, :])

            def x_added(post):
                return lambda k: dve.wait_ge(x_ready, KT * post + k + 1)

            def scale_tables(layer):
                dve.wait_ge(rstd_ready, STATS[f"pre{layer}"] + 1)
                dve.wait_ge(tables, 2 * layer + 2)
                for table in (cos_sb, sin_sb):
                    nc.vector.tensor_tensor(table[:, 0, :], table[:, 0, :], rstd[:, :],
                                            ALU.mult).then_inc(tables_scaled, 1)
                dve.wait_ge(tables_scaled, 2 * layer + 2)

            def reduced_angles(layer):
                inv = C_INV1 if layer else C_INV0
                angle, turns, r = y_sb[:, 0, :], y_sb[:, 1, :], y_sb[:, 2, :]
                step(nc.vector.tensor_scalar(angle, posf[:, :], cst[:, inv:inv + 1], None, ALU.mult))
                step(nc.vector.tensor_scalar(turns, angle, 1.0 / (2 * math.pi), None, ALU.mult))
                step(nc.vector.tensor_scalar(turns, turns, 12582912.0, None, ALU.add))
                step(nc.vector.tensor_scalar(turns, turns, -12582912.0, None, ALU.add))
                for part in two_pi_parts():
                    step(nc.vector.scalar_tensor_tensor(angle, turns, -part, angle, ALU.mult, ALU.add))
                nc.vector.tensor_scalar(r, angle, 3.1415925, -3.1415925, ALU.min, ALU.max).then_inc(angles, 1)
                dve.wait_ge(angles, 2 * layer + 1)
                step(nc.vector.scalar_tensor_tensor(turns, r, -1.0, r, ALU.mult, ALU.max))
                nc.vector.tensor_scalar(y_sb[:, 3, :], turns, -1.0, math.pi / 2, ALU.mult, ALU.add).then_inc(angles, 1)

            def attention(a, take, probs, *events):
                mids = 0

                def mid(ins):
                    nonlocal mids
                    mids += 1
                    ins.then_inc(a.mid, 1)
                    dve.wait_ge(a.mid, mids)

                for t in range(a.n + max([1] + [e[0] for e in events]) + 1):
                    if t < a.n:
                        dve.wait_ge(a.scores, t + 1)
                        take(a, t, mid)
                    if 1 <= t <= a.n:
                        probs(a, t - 1, mid)
                    for after, event in events:
                        h, off = divmod(t - after, a.steps)
                        if off == 0 and 1 <= h <= a.heads:
                            event(h - 1)

            def take_max(width, count, scale):
                def take(a, t, mid):
                    b = a.score_bank(t)
                    mid(nc.vector.tensor_reduce(small[:, t % 2, 0:count], ps[:, b:b + count, 0:width], AX.X, ALU.max))
                    nc.vector.tensor_scalar(small[:, t % 2, 2:2 + count], small[:, t % 2, 0:count], -scale, None,
                                            ALU.mult).then_inc(a.taken, 1)
                return take

            def take_masked(a, t, mid):
                if t >= 3:
                    dve.wait_ge(a.turned, t - 2)
                w, b = a.blocks * P, a.score_bank(t)
                mid(nc.vector.tensor_tensor_reduce(
                    out=a.e[:, t % 3, 0:w], in0=ps[:, b:b + 2, :].rearrange("p b c -> p (b c)")[:, 0:w],
                    in1=mask[:, t % DIL, :], scale=DB_DH ** -0.5, scalar=-3.0e38, op0=ALU.add, op1=ALU.max,
                    accum_out=small[:, t % 2, 0:1]))
                nc.vector.tensor_scalar(small[:, t % 2, 2:3], small[:, t % 2, 0:1], -1.0, None,
                                        ALU.mult).then_inc(a.taken, 1)

            def probs_plain(a, t, mid):
                dve.wait_ge(a.exps, t + 1)
                mid(nc.vector.reciprocal(small[:, t % 2, 6:7], small[:, t % 2, 4:5]))
                e = a.e[:, t % (a.lag + 1), 0:a.blocks * P]
                nc.vector.tensor_scalar(e, e, small[:, t % 2, 6:7], None, ALU.mult).then_inc(a.probs, 1)

            def probs_diff(a, t, mid):
                s = small[:, t % 2]
                e = a.e[:, t % 3]
                dve.wait_ge(a.exps, 2 * t + 2)
                mid(nc.vector.reciprocal(s[:, 6:8], s[:, 4:6]))
                mid(nc.vector.tensor_scalar(s[:, 7:8], s[:, 7:8], lam_w[:, 5:6], None, ALU.mult))
                mid(nc.vector.tensor_scalar(e[:, S:2 * S], e[:, S:2 * S], s[:, 7:8], None, ALU.mult))
                nc.vector.scalar_tensor_tensor(e[:, 0:S], e[:, 0:S], s[:, 6:7], e[:, S:2 * S], ALU.mult,
                                               ALU.add).then_inc(a.probs, 1)

            dve.wait_ge(gain_loaded, 16)
            rests_of(0)
            renew0 = lambda i: renew("pre0", 0, "mix_pre_g", i, lambda k: dve.wait_ge(x_loaded[k // 2], 16))
            for i in range(3):
                renew0(i)
            rests_of(1)
            for i in range(3, KT + 2):
                renew0(i)

            def angles_between(layer):
                def between(j):
                    if j != 0:
                        return
                    if layer == 0:
                        prepare()
                    reduced_angles(layer)
                return between

            def prepare():
                nonlocal steps
                dve.wait_ge(small_loaded, 64)
                nc.vector.tensor_copy(posf[:, :], half[:, 0, :].bitcast(i32)).then_inc(dve_step, 1)
                steps += 1
                nc.vector.tensor_scalar(subg[:, 1:2], subg[:, 0:1], 1.0 - LAMBDA_INIT, None, ALU.mult)
                step(nc.vector.tensor_tensor(lam_sb[:, 0, :], lam_sb[:, 0, :], lam_sb[:, 1, :], ALU.mult))
                step(nc.vector.tensor_tensor(lam_sb[:, 2, :], lam_sb[:, 2, :], lam_sb[:, 3, :], ALU.mult))
                for n in range(2):
                    nc.vector.tensor_reduce(lam_w[:, n:n + 1], lam_sb[:, 2 * n, :], AX.X, ALU.add).then_inc(lam_sums, 1)
                dve.wait_ge(constants, 4)
                step(nc.vector.tensor_reduce(phase4[:, :], ident[:, :].rearrange("p (a b) -> p b a", b=DIL), AX.X, ALU.add))
                nc.vector.tensor_scalar(phase4[:, :], phase4[:, :], -MASKED, MASKED, ALU.mult,
                                        ALU.add).then_inc(phase_ready, 1)

            u = UNITS["qkv0"]
            for n in range(4):
                dst = q0 if n < 2 else k0
                rope_banks(u + n, lambda m, dst=dst, n=n: dst[:, 4 * (n % 2) + m:4 * (n % 2) + m + 1, :],
                           4 * n, DA_DQ // 2, layer=0 if n == 0 else None, done=3 if n else 2, ahead=3,
                           between=angles_between(0) if n == 0 else None)
            unit(u + 4, done=3)
            unit(u + 5)
            dve.wait_ge(lam_exp, 1)
            step(nc.vector.tensor_tensor(lam_w[:, 4:5], lam_w[:, 3:4], lam_w[:, 2:3], ALU.subtract))
            step(nc.vector.tensor_scalar(lam_w[:, 5:6], lam_w[:, 4:5], -LAMBDA_INIT, None, ALU.add))

            def diff_scale(h):
                dve.wait_ge(sub_rstd, h + 1)
                nc.vector.scalar_tensor_tensor(y_sb[:, h, :], y_sb[:, h, :], subg[:, 1:2], half[:, h % 2, :],
                                               ALU.mult, ALU.mult).then_inc(sub_y, 1)

            def diff_rest(h):
                rest("o0", h, act_lo[:, h, :], act_hi[:, h, :], y_sb[:, h, :])

            attention(att_d, take_max(S, 2, DA_DQ ** -0.5), probs_diff, (6, diff_scale), (8, diff_rest))

            def by_token(ap):
                return ap.rearrange("p (l r) -> p r l", r=DIL)

            def dilated_rest(h):
                k = HALF + h
                rest("o1", k, by_token(act_lo[:, k, :]), by_token(act_hi[:, k, :]),
                     ps[:, 6 + h % 2, :].rearrange("p (r l) -> p r l", r=DIL))

            def first_half_rest(k):
                def event(h):
                    if h == 0:
                        rest("o1", k, act_lo[:, k, :], act_hi[:, k, :], y_sb[:, k, :])
                return event

            for layer in range(2):
                if layer == 1:
                    for h in range(2):
                        u = UNITS["qkv1a" if h == 0 else "qkv1b"]
                        n0 = 16 + 8 * GROUPS * h

                        def rope(kind, g, ii, **kw):
                            rope_banks(u + kind, lambda m: (k1 if kind % 2 else q1)[:, g, m, :],
                                       n0 + 4 * kind, DB_DH // 2, ii, **kw)

                        if h == 0:
                            rope(0, slice(0, 1), 0, layer=1, between=angles_between(1))
                        else:
                            rope(0, slice(0, 1), 0)
                        with dve.Fori(0, GROUPS - 1) as g:
                            rope(1, bass.ds(g, 1), g)
                            rope(2, bass.ds(g + 1, 1), g)
                        rope(2 * GROUPS - 1, slice(GROUPS - 1, GROUPS), 0)
                        for g in range(GROUPS):
                            unit(u + 2 * GROUPS + g)
                        if h == 0:
                            dve.wait_ge(mask_step, MASK_STEPS)
                            attention(att_l[h], take_masked, probs_plain)
                        else:
                            attention(att_l[h], take_masked, probs_plain, (2, dilated_rest),
                                      *[(k - 2, first_half_rest(k)) for k in range(HALF)])

                u = UNITS[f"o{layer}"]

                def mem_rests(j):
                    if j == 0:
                        dve.wait_ge(rstd_ready, STATS[f"mem{layer}"] + 1)
                        mem_tile(layer, 0)
                    for i in (2 * j + 1, 2 * j + 2):
                        mem_tile(layer, i)

                unit(u)
                unit(u + 1, between=mem_rests)
                u = UNITS[f"kv{layer}"]
                dve.wait_ge(rstd_ready, STATS[f"mix{layer}"] + 1)
                for n in range(4):
                    unit(u + n, between=lambda j, n=n: renew(
                        f"xpre{layer}", layer, "xa_pre_g", 4 * n + j, x_added(3 * layer), (layer, "mix_post_g"), 2))
                u = UNITS[f"xq{layer}"]
                for n in range(2):
                    def queries(m, n=n):
                        if n == 0 and m == 0:
                            dve.wait_ge(rstd_ready, STATS[f"xpre{layer}"] + 1)
                        dve.wait_ge(bank_done, 4 * (u + n) + m + 1)
                        nc.vector.tensor_tensor(xq[:, 4 * n + m, :], ps[:, 4 * ((u + n) % 2) + m, :], rstd[:, :],
                                                ALU.mult).then_inc(bank_out[(u + n) % 2], 1)
                    unit(u + n, queries)

                def head_rests(h):
                    for k in range(XB * h, XB * (h + 1)):
                        rest(f"xo{layer}", k, act_lo[:, k, :], act_hi[:, k, :], ps[:, 6 + k % XB, :])

                attention(att_x[layer], take_max(MEM, 1, XA_DH ** -0.5), probs_plain, (3, head_rests))
                for n in range(2):
                    unit(UNITS[f"xo{layer}"] + n)
                dve.wait_ge(rstd_ready, STATS[f"xa{layer}"] + 1)
                for i in range(KT + 2):
                    renew(f"fpre{layer}", layer, "ffn_pre_g", i, x_added(3 * layer + 1), (layer, "xa_post_g"))

                u, first, split = UNITS[f"ff{layer}"], STAGED[f"ff{layer}"], SPLITS[f"ff{layer}"]

                def relus_of(up, c, index=0):
                    def bank(m):
                        n = 4 * up + m
                        dve.wait_ge(bank_done, c * 16 + (4 * (u + up) + m + 1))
                        dve.wait_ge(staged, c * KT + (first + n - 1))
                        nc.vector.scalar_tensor_tensor(half[:, n % 2, :], ps[:, 4 * ((u + up) % 2) + m, :], 0.0,
                                                       rstd[:, :], ALU.max, ALU.mult
                                                       ).then_inc(bank_out[(u + up) % 2], 1)
                        if n >= 1:
                            square_rest(n - 1, c)
                    return bank

                def square_rest(n, c):
                    dve.wait_ge(hi_ready, c * KT + (split + n + 1))
                    nc.vector.tensor_tensor(ff_lo[:, n, :], stage[:, n % 2, :], ff_hi[:, n, :].bitcast(f32),
                                            ALU.subtract).then_inc(lo_ready, 1)

                def share_of(down, c):
                    v = u + 2 + down

                    def bank(m):
                        tile = y_sb[:, 4 * down + m, :]
                        dve.wait_ge(bank_done, c * 16 + (4 * v + m + 1))
                        dve.wait_ge(bank_out[v % 2], banks_out(v - 2, m, c * 2))
                        nc.vector.tensor_tensor(tile, ps[:, 4 * (v % 2) + m, :], tile,
                                                ALU.add).then_inc(bank_out[v % 2], 1)
                    return bank

                def first_bank(m):
                    if m == 0:
                        dve.wait_ge(rstd_ready, STATS[f"fpre{layer}"] + 1)
                    relus_of(0, 0)(m)

                unit(u, first_bank)
                dve.wait_ge(y_cleared, layer + 1)
                with dve.Fori(0, CHUNKS - 1) as c:
                    unit(u + 1, relus_of(1, c), c * 2)
                    square_rest(KT - 1, c)
                    unit(u + 2, share_of(0, c), c * 2)
                    unit(u + 3, share_of(1, c), c * 2)
                    unit(u + 4, relus_of(0, c + 1), c * 2)
                c = CHUNKS - 1
                unit(u + 4 * c + 1, relus_of(1, c))
                square_rest(KT - 1, c)
                unit(u + 4 * c + 2, share_of(0, c))
                unit(u + 4 * c + 3, share_of(1, c))
                dve.wait_ge(rstd_ready, STATS[f"ff{layer}"] + 1)
                for i in range(KT + 2):
                    renew("pre1" if layer == 0 else None, 1, "mix_pre_g", i, x_added(3 * layer + 2),
                          (layer, "ffn_post_g"))

        @block.tensor
        def _(pe):
            def unit(u, hi, lo, split, ii=0, split_ii=0, tokens=None, nb=4, width=NB, last_bank=None, before=None):
                s = 4 * (u % 2)
                if u >= 2:
                    pe.wait_ge(bank_out[u % 2], ii * 4 + 4 * (u // 2))
                for j in range(4):
                    if j == 3 and before:
                        before()
                    pe.wait_ge(w_lo_ready, ii * 8 + (4 * u + j + 1))
                    for a in range(2):
                        k = 2 * j + a
                        pe.wait_ge(lo_ready, split_ii * KT + (split + k + 1))
                        for m in range(nb):
                            if last_bank and k == 0 and m == 3:
                                last_bank()
                            wh, wl = w_hi[:, j % 2, a], w_lo[:, j % 2, a]
                            if tokens is None:
                                c = slice(m * P, (m + 1) * P)
                                passes = ((wl[:, c], hi[:, k]), (wh[:, c], lo[:, k]), (wh[:, c], hi[:, k]))
                            else:
                                th, tl = tokens(hi[:, k], m), tokens(lo[:, k], m)
                                passes = ((tl, wh), (th, wl), (th, wh))
                            for n, (left, right) in enumerate(passes):
                                last = nc.tensor.matmul(ps[:, s + m, 0:width], left, right,
                                                        start=(k == 0 and n == 0), stop=(k == KT - 1 and n == 2))
                            if k == KT - 1:
                                last.then_inc(bank_done, 4 // nb)
                    if j < 3:
                        last.then_inc(pair_used, 1)

            def natural(ap, m):
                return ap[:, m * P:(m + 1) * P]

            def statistic(name, part=None, squares=sq):
                v, width = STAT_BEFORE[name], squares.shape[-1]
                bank = ps[:, stat_bank(name), 0:width]
                if part != 1:
                    if v >= 2:
                        pe.wait_ge(bank_out[v % 2], 4 * (v // 2))
                    pe.wait_ge(sq_summed, summed(name))
                    last = nc.tensor.matmul(bank, ones[:, :], squares[:, 0, :], start=True, stop=(part is None))
                if part == 1:
                    for k in range(4, KT):
                        pe.wait_ge(sq_ready, KT * STATS[name] + k + 1)
                        last = nc.tensor.matmul(bank, ones[:, :], squares[:, k, :], start=False, stop=(k == KT - 1))
                if part != 0:
                    last.then_inc(stat_done, 1)

            def sums_read(name):
                return lambda: pe.wait_ge(ln_done, STATS[name] + 1)

            def columns(v, n):
                pe.wait_ge(bank_out[v % 2], 4 * (v // 2))
                for j in range(2 * DIL):
                    tile = rstd[0:1, :]
                    tile = natural(tile, j) if j < DIL else residue(tile, j - DIL)
                    last = nc.tensor.matmul(ps[:, 4 * (v % 2) + 3, j:j + 1], tile, ones[0:1, 0:1],
                                            start=True, stop=True)
                last.then_inc(cols_done, 1)
                return lambda: pe.wait_ge(cols_read, n)

            def attention(a, scores, scores_read, per_step, weigh, o_free, head_stat=None):
                for t in range(a.n + a.lag + 3):
                    if t < a.n:
                        if t >= a.depth:
                            pe.wait_ge(scores_read, per_step * (t - a.depth + 1))
                        scores(t // a.steps, t % a.steps, t).then_inc(a.scores, 1)
                    if a.lag <= t < a.n + a.lag:
                        n = t - a.lag
                        pe.wait_ge(a.probs, n + 1)
                        copied = n if a.single else n - 1
                        if copied > 0:
                            pe.wait_ge(a.pT, copied)
                        for b in range(a.blocks):
                            last = nc.tensor.transpose(a.turn_banks(n, b),
                                                       a.e[:, n % (a.lag + 1), b * P:(b + 1) * P], ident[:, :])
                        last.then_inc(a.turned, 1)
                    if a.lag < t <= a.n + a.lag:
                        n = t - a.lag - 1
                        pe.wait_ge(a.pT, n + 1)
                        if n % a.steps == 0:
                            o_free(n // a.steps)
                        weigh(n // a.steps, n % a.steps, n).then_inc(a.weighed, 1)
                    h, off = divmod(t - 4, a.steps)
                    if head_stat and off == 0 and 1 <= h <= a.heads:
                        head_stat(h - 1)

            def o_read(a):
                def o_free(h):
                    if h >= 2:
                        pe.wait_ge(a.o_out, h - 1)
                return o_free

            def p_of(a, n, b):
                return a.p[:, n % 2, b * P:(b + 1) * P]

            pe.wait_ge(constants, 4)
            u = UNITS["qkv0"]
            for n in range(4):
                unit(u + n, act_hi, act_lo, SPLITS["pre0"], before=(lambda: statistic("pre0")) if n == 0 else None,
                     last_bank=sums_read("pre0") if n == 1 else None)
            pe.wait_ge(rstd_ready, STATS["pre0"] + 1)
            read = columns(u + 4, 1)
            for n in range(2):
                unit(u + 4 + n, act_hi, act_lo, SPLITS["pre0"], tokens=natural, last_bank=read if n == 0 else None)

            pe.wait_ge(rope_done, 16)
            for n in range(2):
                pe.wait_ge(bank_out[(u + 4 + n) % 2], banks_out(u + 4 + n, 3))

            def scores_diff(h, s, t):
                for c in range(2):
                    r = slice(c * DA_DQ, (c + 1) * DA_DQ)
                    last = nc.tensor.matmul(ps[:, 2 * (t % 2) + c, :], q0[r, h, s * P:(s + 1) * P], k0[r, h, :],
                                            start=True, stop=True)
                return last

            def weigh_diff(h, s, n):
                for b in range(S // P):
                    last = nc.tensor.matmul(ps[:, 6 + h % 2, s * P:(s + 1) * P], v0[:, b, h * P:(h + 1) * P],
                                            p_of(att_d, n, b), start=(b == 0), stop=(b == S // P - 1))
                return last

            def head_stat(h):
                pe.wait_ge(sub_sq, h + 1)
                if h >= 1:
                    pe.wait_ge(sub_ln, h)
                nc.tensor.matmul(ps[:, 5, :], ones[:, :], stage[:, h % 2, :], start=True,
                                 stop=True).then_inc(sub_stat, 1)

            attention(att_d, scores_diff, att_d.exps, 2, weigh_diff, o_read(att_d), head_stat)
            pe.wait_ge(att_d.o_out, DA_HEADS)

            for layer in range(2):
                if layer == 1:
                    split = SPLITS["pre1"]
                    for h in range(2):
                        u = UNITS["qkv1a" if h == 0 else "qkv1b"]
                        unit(u, act_hi, act_lo, split, last_bank=sums_read("ff0") if h == 0 else None,
                             before=(lambda: statistic("pre1")) if h == 0 else None)
                        with pe.Fori(0, GROUPS - 1) as g:
                            unit(u + 1, act_hi, act_lo, split, g, last_bank=sums_read("pre1"))
                            unit(u + 2, act_hi, act_lo, split, g)
                        unit(u + 2 * GROUPS - 1, act_hi, act_lo, split)
                        read = columns(u + 2 * GROUPS, 2) if h == 0 else None
                        for g in range(GROUPS):
                            unit(u + 2 * GROUPS + g, act_hi, act_lo, split, tokens=natural if g == 0 else residue,
                                 last_bank=read if g == 0 else None)
                        pe.wait_ge(rope_done, 16 + 8 * GROUPS * (h + 1))
                        for g in range(GROUPS):
                            v = u + 2 * GROUPS + g
                            pe.wait_ge(bank_out[v % 2], banks_out(v, 3))

                        def scores_dilated(h, r, t):
                            b = 2 * (t % 2)
                            nc.tensor.matmul(ps[:, b, :], residue(q1[:, 0, h, :], r), k1[:, 0, h, :],
                                             start=True, stop=True)
                            for g in (1, 2):
                                last = nc.tensor.matmul(ps[:, b + 1, (g - 1) * P:g * P], residue(q1[:, g, h, :], r),
                                                        residue(k1[:, g, h, :], r), start=True, stop=True)
                            return last

                        def weigh_dilated(h, r, n):
                            for b in range(S // P + 2):
                                g, tile = (0, b) if b < S // P else (b - S // P + 1, r)
                                last = nc.tensor.matmul(ps[:, 6 + h % 2, r * P:(r + 1) * P],
                                                        v1[:, g, tile, h * P:(h + 1) * P], p_of(att_l[0], n, b),
                                                        start=(b == 0), stop=(b == S // P + 1))
                            return last

                        if h == 0:
                            attention(att_l[h], scores_dilated, att_l[h].taken, 1, weigh_dilated, o_read(att_l[h]))
                            pe.wait_ge(att_l[h].o_out, HALF)
                        else:
                            def o_split(head):
                                if head >= 2:
                                    pe.wait_ge(lo_ready, SPLITS["o1"] + HALF + head - 1)
                            attention(att_l[h], scores_dilated, att_l[h].taken, 1, weigh_dilated, o_split)

                o = UNITS[f"o{layer}"]
                split = SPLITS[f"o{layer}"]
                if layer == 0:
                    pe.wait_ge(sub_ln, DA_HEADS)
                unit(o, act_hi, act_lo, split, before=lambda: statistic(f"mem{layer}", squares=mem_sq))
                unit(o + 1, act_hi, act_lo, split, last_bank=sums_read(f"mem{layer}"), before=lambda: statistic(f"mix{layer}", 0))
                statistic(f"mix{layer}", 1)
                u = UNITS[f"kv{layer}"]
                split = SPLITS[f"mem{layer}"]
                for n in range(2):
                    unit(u + n, mem_hi, mem_lo, split, tokens=natural, nb=2)
                for n in range(2, 4):
                    unit(u + n, mem_hi, mem_lo, split, width=MEM, last_bank=sums_read(f"mix{layer}"),
                         before=(lambda: statistic(f"xpre{layer}")) if n == 3 else None)
                u = UNITS[f"xq{layer}"]
                unit(u, act_hi, act_lo, SPLITS[f"xpre{layer}"], last_bank=sums_read(f"xpre{layer}"))
                unit(u + 1, act_hi, act_lo, SPLITS[f"xpre{layer}"])

                for n in range(4):
                    v = UNITS[f"kv{layer}"] + n
                    pe.wait_ge(bank_out[v % 2], banks_out(v, 3))

                def scores_cross(h, s, t):
                    v, m = divmod(XB * h + XB - 1, 4)
                    pe.wait_ge(bank_out[(u + v) % 2], banks_out(u + v, m))
                    for b in range(XB):
                        last = nc.tensor.matmul(ps[:, a.score_bank(t), 0:MEM], xq[:, XB * h + b, s * P:(s + 1) * P],
                                                xk[:, XB * h + b, :], start=(b == 0), stop=(b == XB - 1))
                    return last

                def weigh_cross(h, s, n):
                    for d in range(XB):
                        for b in range(MEM // P):
                            c = (XB * h + d) * P
                            last = nc.tensor.matmul(ps[:, 6 + d, s * P:(s + 1) * P], xv[:, b, c:c + P], p_of(a, n, b),
                                                    start=(b == 0), stop=(b == MEM // P - 1))
                    return last

                def split_read(h):
                    if h >= 1:
                        pe.wait_ge(lo_ready, SPLITS[f"xo{layer}"] + XB * h)

                a = att_x[layer]
                attention(a, scores_cross, a.exps, 1, weigh_cross, split_read)
                u = UNITS[f"xo{layer}"]
                unit(u, act_hi, act_lo, SPLITS[f"xo{layer}"])
                unit(u + 1, act_hi, act_lo, SPLITS[f"xo{layer}"], before=lambda: statistic(f"xa{layer}", 0))
                statistic(f"xa{layer}", 1)

                u = UNITS[f"ff{layer}"]
                up = (act_hi, act_lo, SPLITS[f"fpre{layer}"])
                down = (ff_hi, ff_lo, SPLITS[f"ff{layer}"])
                unit(u, *up, last_bank=sums_read(f"xa{layer}"), before=lambda: statistic(f"fpre{layer}"))
                with pe.Fori(0, CHUNKS - 1) as c:
                    unit(u + 1, *up, c * 2, last_bank=sums_read(f"fpre{layer}"))
                    unit(u + 2, *down, c * 2, split_ii=c)
                    unit(u + 3, *down, c * 2, split_ii=c)
                    unit(u + 4, *up, c * 2)
                c = CHUNKS - 1
                unit(u + 4 * c + 1, *up)
                unit(u + 2, *down, c * 2, split_ii=c)
                unit(u + 3, *down, c * 2, split_ii=c, before=lambda: statistic(f"ff{layer}", 0))
                statistic(f"ff{layer}", 1)


MASK_STEPS = 1 + DIL * 6


def kernel(**inputs):
    import concourse.bacc as _bacc
    from concourse.bass_utils import run_bass_kernel_spmd as _run

    def lay(a, features=True):
        return np.ascontiguousarray(a.T.reshape(-1, P, a.shape[0]).transpose(1, 0, 2))

    a = {name: np.asarray(value) for name, value in inputs.items()}
    gains = np.stack([a[name][layer] for layer in range(2) for name in LAYER_GAINS])
    arrays = {
        "x": lay(a["x"][0]),
        "mem": lay(a["mem"][0]),
        "positions": np.ascontiguousarray(a["positions"]),
        "gains": np.ascontiguousarray(gains.reshape(len(gains), KT, P).transpose(2, 0, 1)),
        "consts": rope_columns(),
        "lam": np.ascontiguousarray(a["da_lambda"].reshape(1, -1)),
        "subln_g": np.ascontiguousarray(a["da_subln_g"].reshape(P, 1)),
        "da_w_qkv": a["da_w_qkv"][0], "da_w_o": a["da_w_o"][0],
        "db_w_qkv": a["db_w_qkv"][0], "db_w_o": a["db_w_o"][0],
        "xa_wq": a["xa_wq"], "xa_wkv": a["xa_wkv"], "xa_wo": a["xa_wo"],
        "w_up": a["w_up"], "w_down": a["w_down"],
    }
    nc = _bacc.Bacc("TRN2", target_bir_lowering=False, num_devices=1)
    aps = {}
    for name, value in arrays.items():
        aps[name] = nc.dram_tensor(f"in_{name}", value.shape, mybir.dt.from_np(value.dtype), kind="ExternalInput").ap()
    out = nc.dram_tensor("out_0", (P, KT, S), mybir.dt.float32, kind="ExternalOutput").ap()
    build(nc, out=out, **aps)
    r = _run(nc, [{f"in_{name}": value for name, value in arrays.items()}], core_ids=[0])
    y = r.results[0]["out_0"]
    return np.ascontiguousarray(y.transpose(2, 1, 0).reshape(1, S, D))
```

```python
import math
from contextlib import ExitStack

import numpy as np

import concourse.bass as bass
from concourse import mybir

D = 1024
S = 512
MEM = 256
P = 128
KT = D // P
NB = 512
EPS = 1e-6
THETA = 10000.0
DA_HEADS, DA_DQ = 8, 64
LAMBDA_INIT = 0.8 - 0.6 * math.exp(-0.3 * 0)
GROUPS, DB_DH = 3, 128
HALF = 4
DIL = 4
RADIUS = 64
XA_HEADS, XA_DH = 4, 256
XB = XA_DH // P
FF = 4 * D
CHUNKS = FF // D
MASKED = -1.0e37
LAYER_GAINS = ["mix_pre_g", "mix_post_g", "xa_pre_g", "mem_g", "xa_post_g", "ffn_pre_g", "ffn_post_g"]

C_INV0, C_SIGN0, C_INV1, C_SIGN1 = range(4)


def rope_columns():
    cols = np.zeros((P, 4), np.float32)
    for at, dh in ((0, DA_DQ), (2, DB_DH)):
        inv = np.float32(THETA) ** (-np.arange(0, dh, 2, dtype=np.float32) / np.float32(dh))
        row = np.arange(P) % dh
        cols[:, at] = inv.astype(np.float32)[row % (dh // 2)]
        cols[:, at + 1] = np.where(row < dh // 2, 1.0, -1.0)
    return cols


def two_pi_parts():
    parts, rest = [], 2 * math.pi
    for bits in (8, 9, 9):
        e = math.floor(math.log2(rest)) - bits + 1
        part = math.floor(rest / 2.0**e) * 2.0**e
        parts.append(part)
        rest -= part
    return parts + [rest]


def numbered(names, sizes):
    at, n = {}, 0
    for name, size in zip(names, sizes):
        at[name] = n
        n += size
    return at, n


UNITS, TOTAL_UNITS = numbered(
    ["qkv0", "o0", "kv0", "xq0", "xo0", "ff0", "qkv1a", "qkv1b", "o1", "kv1", "xq1", "xo1", "ff1"],
    [6, 2, 4, 2, 2, 4 * CHUNKS, 3 * GROUPS, 3 * GROUPS, 2, 4, 2, 2, 4 * CHUNKS])
SPLIT_NAMES = ["pre0", "o0", "mem0", "xpre0", "xo0", "fpre0", "ff0", "pre1", "o1", "mem1", "xpre1", "xo1",
               "fpre1", "ff1"]
SPLITS, _ = numbered(SPLIT_NAMES, [KT * CHUNKS if n.startswith("ff") else KT for n in SPLIT_NAMES])
STAGED_NAMES = [n for n in SPLIT_NAMES if n not in ("o0", "xo0", "o1", "xo1")]
STAGED, _ = numbered(STAGED_NAMES, [KT * CHUNKS if n.startswith("ff") else KT for n in STAGED_NAMES])
STAT_NAMES = ["pre0", "mem0", "mix0", "xpre0", "xa0", "fpre0", "ff0",
              "pre1", "mem1", "mix1", "xpre1", "xa1", "fpre1", "ff1"]
STATS, _ = numbered(STAT_NAMES, [1] * len(STAT_NAMES))
STAT_BEFORE = {"pre0": UNITS["qkv0"] + 1, "ff0": UNITS["qkv1a"], "pre1": UNITS["qkv1a"] + 1, "ff1": TOTAL_UNITS}
for _l in "01":
    STAT_BEFORE.update({"mem" + _l: UNITS["o" + _l] + 1, "mix" + _l: UNITS["kv" + _l], "xpre" + _l: UNITS["xq" + _l] + 1,
                        "xa" + _l: UNITS["ff" + _l], "fpre" + _l: UNITS["ff" + _l] + 1})


PLAN = [(None, None), (None, None), (0, None), (1, None), (None, 0), (2, None), (None, 1), (3, None), (None, 2),
        (4, None), (None, 3), (5, None), (None, 4), (6, None), (None, 5), (7, None),
        (None, 6), (None, 7), (None, 8)]
FIRST_PLANNED = PLAN.index((0, None))

X_LOADS = [(0, 1), (1, 2)] + [(k, k + 2) for k in range(2, KT, 2)]

ADDED_BY_DVE = [(), (0,), (0,), (), (0,), (0, 2, 5, 7)]


def additions(post, k):
    by_dve = k in ADDED_BY_DVE[post]
    tiles = [(p, i) for p in range(post + 1) for i in range(KT) if p < post or i <= k]
    return by_dve, sum((i in ADDED_BY_DVE[p]) == by_dve for p, i in tiles)


BOUNDARY_TILES = 4

POOLED = {n: 6 if n[:2] in ("xa", "ff") else KT for n in STAT_NAMES}


def summed(name, k=None):
    before = sum(POOLED[n] - 1 for n in STAT_NAMES[:STATS[name]])
    return before + (POOLED[name] - 1 if k is None else k)


def stat_bank(name):
    return 4 * (STAT_BEFORE[name] % 2) + 3


def banks_out(u, m, ii=0, nb=4):
    return ii * 4 + (4 * (u // 2) + (m + 1) * (4 // nb))


def residue(ap, r):
    return ap.rearrange("p (l r) -> p r l", r=DIL)[:, r]


def build(nc, x, mem, positions, gains, consts, lam, subln_g, da_w_qkv, da_w_o, db_w_qkv, db_w_o,
          xa_wq, xa_wkv, xa_wo, w_up, w_down, out):
    f32, f32r, bf16, i32 = mybir.dt.float32, mybir.dt.float32r, mybir.dt.bfloat16, mybir.dt.int32
    ACT = mybir.ActivationFunctionType
    ALU = mybir.AluOpType
    AX = mybir.AxisListType

    def tiles(w):
        return w.rearrange("(r a p) (n c) -> r n p a c", a=2, p=P, c=NB)

    with ExitStack() as ctx:
        def sb(name, shape, dt=f32, scope=ctx):
            return scope.enter_context(nc.sbuf_tensor(name, shape, dt))

        def sem(name):
            return ctx.enter_context(nc.semaphore(name))

        x_sb = sb("x_sb", [P, KT, S])
        y_sb = sb("y_sb", [P, KT, S])
        act_hi = sb("act_hi", [P, KT, S], f32r)
        act_lo = sb("act_lo", [P, KT, S], f32r)
        raw = sb("raw", [P, 4, 2, NB])
        w_hi = sb("w_hi", [P, 2, 2, NB], f32r)
        w_lo = sb("w_lo", [P, 2, 2, NB], f32r)
        cos_sb = sb("cos_sb", [P, 1, S])
        sin_sb = sb("sin_sb", [P, 1, S])
        posf = sb("posf", [P, S])
        mask = sb("mask", [P, DIL, S + 2 * P], bf16)
        stage = sb("stage", [P, 2, S])
        half = sb("half", [P, 2, S])
        rstd = sb("rstd", [P, S])
        gain = sb("gain", [P, 2 * len(LAYER_GAINS), KT])
        cst = sb("cst", [P, 4])
        lam_sb = half[:, 1, 0:4 * DA_DQ].rearrange("p (a b) -> p a b", a=4)
        lam_w = sb("lam_w", [P, 8])
        subg = sb("subg", [P, 2])
        ones = sb("ones", [P, P])
        ident = sb("ident", [P, P])
        phase4 = sb("phase4", [P, DIL])
        eps = sb("eps", [P, 1])
        rstd_cols = sb("rstd_cols", [P, 2 * DIL])
        small = sb("small", [P, 2, 8])
        with ExitStack() as scope:
            e_sb = sb("e_sb", [P, 3, 1024], scope=scope)
            pT_sb = sb("pT_sb", [P, 2, S], scope=scope)
        with ExitStack() as scope:
            el_sb = sb("el_sb", [P, 3, S + 2 * P], scope=scope)
            plT_sb = sb("plT_sb", [P, 2, S + 2 * P], scope=scope)
        with ExitStack() as scope:
            ex_sb = sb("ex_sb", [P, 4, MEM], scope=scope)
            pxT_sb = sb("pxT_sb", [P, 2, MEM], scope=scope)
        sq = sb("sq", [P, KT, S])
        with ExitStack() as scope:
            q0 = sb("q0", [P, DA_HEADS, S], scope=scope)
            k0 = sb("k0", [P, DA_HEADS, S], scope=scope)
            v0 = sb("v0", [P, S // P, D], scope=scope)
        with ExitStack() as scope:
            q1 = sb("q1", [P, GROUPS, HALF, S], scope=scope)
            k1 = sb("k1", [P, GROUPS, HALF, S], scope=scope)
            v1 = sb("v1", [P, GROUPS, S // P, HALF * P], scope=scope)
        with ExitStack() as scope:
            xq = sb("xq", [P, KT, S], scope=scope)
            xk = sb("xk", [P, KT, MEM], scope=scope)
            xv = sb("xv", [P, MEM // P, D], scope=scope)
            mem_sb = sb("mem_sb", [P, KT, MEM], scope=scope)
            mem_hi = sb("mem_hi", [P, KT, MEM], f32r, scope=scope)
            mem_lo = sb("mem_lo", [P, KT, MEM], f32r, scope=scope)
            mem_sq = sb("mem_sq", [P, KT, MEM], scope=scope)
        with ExitStack() as scope:
            ff_hi = sb("ff_hi", [P, KT, S], f32r, scope=scope)
            ff_lo = sb("ff_lo", [P, KT, S], f32r, scope=scope)
            angles_sb = sb("angles_sb", [P, 4, S], scope=scope)
        ps = ctx.enter_context(nc.psum_tensor("ps", [P, 8, NB], f32))

        raw_loaded = [sem(f"raw_loaded{j}") for j in range(4)]
        w_hi_ready = sem("w_hi_ready")
        w_lo_ready = sem("w_lo_ready")
        pair_used = sem("pair_used")
        bank_done = sem("bank_done")
        bank_out = [sem("bank_out0"), sem("bank_out1")]
        hi_ready = sem("hi_ready")
        lo_ready = sem("lo_ready")
        staged = sem("staged")
        sq_ready = sem("sq_ready")
        sq_summed = sem("sq_summed")
        stat_done = sem("stat_done")
        ln_done = sem("ln_done")
        rstd_ready = sem("rstd_ready")
        y_scaled = sem("y_scaled")
        x_ready = sem("x_ready")
        x_ready_dve = sem("x_ready_dve")
        y_cleared = sem("y_cleared")
        rope_done = sem("rope_done")
        sub_sq = sem("sub_sq")
        sub_stat = sem("sub_stat")
        sub_ln = sem("sub_ln")
        sub_rstd = sem("sub_rstd")
        sub_y = sem("sub_y")
        cols_done = sem("cols_done")
        cols_read = sem("cols_read")
        tables_scaled = sem("tables_scaled")
        x_loaded = [sem(f"x_loaded{j}") for j in range(len(X_LOADS))]
        gain_loaded = sem("gain_loaded")
        small_loaded = sem("small_loaded")
        mem_loaded = sem("mem_loaded")
        dve_step = sem("dve_step")
        constants = sem("constants")
        phase_ready = sem("phase_ready")
        mask_step = sem("mask_step")
        angles = sem("angles")
        tables = sem("tables")
        lam_sums = sem("lam_sums")
        lam_exp = sem("lam_exp")
        out_done = sem("out_done")

        class Attention:

            def __init__(self, name, heads, blocks, wide=False, narrow=False, first_bank=0):
                self.heads, self.steps, self.blocks = heads, S // P, blocks
                self.first_bank, self.turned_bank = first_bank, 4 - first_bank
                self.narrow = narrow
                self.wide = wide
                self.single = wide
                self.lag = 3 if narrow else 2
                self.n = heads * self.steps
                self.e, self.p = (el_sb, plT_sb) if wide else (ex_sb, pxT_sb) if narrow else (e_sb, pT_sb)
                self.scores = sem(name + "_scores")
                self.taken = sem(name + "_taken")
                self.exps = sem(name + "_exps")
                self.probs = sem(name + "_probs")
                self.mid = sem(name + "_mid")
                self.mids = 0
                self.turned = sem(name + "_turned")
                self.pT = sem(name + "_pT")
                self.weighed = sem(name + "_weighed")
                self.o_out = sem(name + "_o_out")

            def turn_banks(self, n, b):
                if self.wide:
                    return ps[:, self.turned_bank + b // 4, (b % 4) * P:(b % 4 + 1) * P]
                return ps[:, self.turned_bank + n % 2, b * P:(b + 1) * P]

            def turned_all(self, n):
                if self.wide:
                    both = ps[:, self.turned_bank:self.turned_bank + 2, :]
                    return both.rearrange("p b c -> p (b c)")[:, 0:self.blocks * P]
                return ps[:, self.turned_bank + n % 2, 0:self.blocks * P]

            def score_bank(self, t):
                return self.first_bank + 2 * (t % 2)

            def out_bank(self, h):
                return self.turned_bank + 2 + h % 2

            def narrow_scores(self, t):
                return ps[:, t % 2, 0:MEM]

            def cross_bank(self, k):
                return (6 if k // XB % 2 else 2) + k % XB

        att_d = Attention("diff", DA_HEADS, S // P)
        att_l = [Attention(f"dil{h}", HALF, S // P + 2, wide=True, first_bank=4 * (1 - h)) for h in range(2)]
        att_x = [Attention(f"cross{i}", XA_HEADS, MEM // P, narrow=True) for i in range(2)]

        def gcol(layer, name, k):
            n = layer * len(LAYER_GAINS) + LAYER_GAINS.index(name)
            return gain[:, n, k:k + 1]

        def wait_loaded(engine, k):
            for n, (first, end) in enumerate(X_LOADS):
                if first <= k < end:
                    engine.wait_ge(x_loaded[n], 16)

        def wait_added(engine, post, k):
            by_dve, count = additions(post, k)
            engine.wait_ge(x_ready_dve if by_dve else x_ready, count)

        block = ctx.enter_context(nc.Block())

        @block.sync
        def _(sp):
            def load_unit(u, w, row_pair, col, ii=0):
                for j in range(4):
                    if u > 0:
                        sp.wait_ge(w_lo_ready, ii * 8 + (4 * u + j - 3))
                    src = w[bass.ds(row_pair + j, 1), bass.ds(col, 1)]
                    sp.dma_start(raw[:, j], src[0, 0]).then_inc(raw_loaded[j], 16)

            sp.dma_start(gain[:, :, :], gains).then_inc(gain_loaded, 16)
            for n, (k, end) in enumerate(X_LOADS):
                sp.dma_start(x_sb[:, k:end, :], x[:, k:end]).then_inc(x_loaded[n], 16)
                if n == 0:
                    w = tiles(da_w_qkv)
                    load_unit(0, w, 0, 0)
            sp.dma_start(cst[:, :], consts).then_inc(small_loaded, 16)
            sp.dma_start(half[:, 0, :].bitcast(i32), positions.broadcast_to([P, S])).then_inc(small_loaded, 16)
            sp.dma_start(half[:, 1, 0:4 * DA_DQ],
                         lam.broadcast_to([P, 4 * DA_DQ])).then_inc(small_loaded, 16)
            sp.dma_start(subg[:, 0:1], subln_g).then_inc(small_loaded, 16)
            for n in range(1, 6):
                load_unit(n, w, 0, n)

            def after_attention(layer, att):
                u = UNITS[f"o{layer}"]
                w = tiles(da_w_o if layer == 0 else db_w_o)
                load_unit(u, w, 0, 0)
                sp.wait_ge(att.weighed, att.n)
                sp.dma_start(mem_sb[:, :, :], mem).then_inc(mem_loaded, 16)
                load_unit(u + 1, w, 0, 1)
                w = tiles(xa_wkv[layer])
                for n, col in enumerate((2, 3, 0, 1)):
                    load_unit(UNITS[f"kv{layer}"] + n, w, 0, col)
                for name, w in (("xq", xa_wq), ("xo", xa_wo)):
                    for n in range(2):
                        load_unit(UNITS[f"{name}{layer}"] + n, tiles(w[layer]), 0, n)
                u = UNITS[f"ff{layer}"]
                up, down = tiles(w_up[layer]), tiles(w_down[layer])
                load_unit(u, up, 0, 0)
                with sp.Fori(0, CHUNKS - 1) as c:
                    load_unit(u + 1, up, 0, c * 2 + 1, c * 2)
                    for n in range(2):
                        load_unit(u + 2 + n, down, c * 4, n, c * 2)
                    load_unit(u + 4, up, 0, c * 2 + 2, c * 2)
                u += 4 * (CHUNKS - 1)
                load_unit(u + 1, up, 0, 2 * CHUNKS - 1)
                for n in range(2):
                    load_unit(u + 2 + n, down, 4 * (CHUNKS - 1), n)

            after_attention(0, att_d)
            w = tiles(db_w_qkv)
            for h in range(2):
                u = UNITS["qkv1a" if h == 0 else "qkv1b"]
                load_unit(u, w, 0, h)
                with sp.Fori(0, GROUPS - 1) as g:
                    load_unit(u + 1, w, 0, g * 2 + (2 * GROUPS + h), g)
                    load_unit(u + 2, w, 0, g * 2 + (2 + h), g)
                load_unit(u + 2 * GROUPS - 1, w, 0, 4 * GROUPS - 2 + h)
                for g in range(GROUPS):
                    load_unit(u + 2 * GROUPS + g, w, 0, 4 * GROUPS + 2 * g + h)
            after_attention(1, att_l[1])
            for k in range(KT):
                wait_added(sp, 5, k)
                sp.dma_start(out[:, k], x_sb[:, k, :]).then_inc(out_done, 16)
            sp.wait_ge(out_done, 16 * KT)

        @block.gpsimd
        def _(pool):
            sums = 0

            def square_sum(name, k, squares):
                nonlocal sums
                if k == 0:
                    return
                pool.wait_ge(sq_ready, KT * STATS[name] + k + 1)
                pool.wait_ge(sq_summed, sums)
                nc.gpsimd.tensor_tensor(squares[:, 0, :], squares[:, 0, :], squares[:, k, :],
                                        ALU.add).then_inc(sq_summed, 1)
                sums += 1
                assert sums == summed(name, k)

            nc.gpsimd.memset(ones[:, :], 1.0).then_inc(constants, 1)
            nc.gpsimd.memset(eps[:, :], EPS).then_inc(constants, 1)
            nc.gpsimd.memset(ident[:, :], 0.0).then_inc(constants, 1)
            pool.wait_ge(constants, 3)
            nc.gpsimd.affine_select(out=ident[:, :], in_=ident[:, :], compare_op=ALU.not_equal, fill=1.0,
                                    base=0, pattern=[[-1, P]], channel_multiplier=1).then_inc(constants, 1)

            for k in range(KT):
                square_sum("pre0", k, sq)

            nc.gpsimd.memset(mask[:, :, 0:S + P], 0.0).then_inc(mask_step, 1)
            steps = 1
            for r in range(DIL):
                for at, width, step, base in ((0, S, DIL, r), (S, P, 1, 0)):
                    part = mask[:, r, at:at + width]
                    for sign in (1, -1):
                        pool.wait_ge(mask_step, steps)
                        nc.gpsimd.affine_select(out=part, in_=part, compare_op=ALU.is_ge, fill=MASKED,
                                                base=RADIUS - sign * base, pattern=[[sign, width]],
                                                channel_multiplier=-sign * step).then_inc(mask_step, 1)
                        steps += 1
                if r == 0:
                    pool.wait_ge(phase_ready, 1)
                for a in range(2):
                    far = mask[:, r, S + P + a * 64:S + P + (a + 1) * 64].rearrange("p (a b) -> p a b", b=DIL)
                    nc.gpsimd.tensor_copy(far, phase4[:, :].rearrange("p (o b) -> p o b", o=1)
                                          .broadcast_to([P, 16, DIL])).then_inc(mask_step, 1)
                    steps += 1
            assert steps == MASK_STEPS

            def rope_sum(value, parity, dst, n):
                pool.wait_ge(bank_out[parity], value)
                nc.gpsimd.tensor_tensor(dst, dst, half[:, n % 2:n % 2 + 1, :], ALU.add).then_inc(rope_done, 1)

            for n in range(16):
                u = UNITS["qkv0"] + n // 4
                dst = (q0 if n < 8 else k0)[:, n % 8:n % 8 + 1, :]
                rope_sum(banks_out(u, n % 4), u % 2, dst, n)
            def residual_sums(post, name=None):
                for k in range(KT + 2):
                    if k < KT and k not in ADDED_BY_DVE[post]:
                        pool.wait_ge(y_scaled, KT * post + k + 1)
                        nc.gpsimd.tensor_tensor(x_sb[:, k, :], x_sb[:, k, :], y_sb[:, k, :],
                                                ALU.add).then_inc(x_ready, 1)
                    if name and k >= 2:
                        square_sum(name, k - 2, sq)

            for layer in range(2):
                for k in range(KT):
                    square_sum(f"mem{layer}", k, mem_sq)
                for k in range(POOLED[f"mix{layer}"]):
                    square_sum(f"mix{layer}", k, sq)
                residual_sums(3 * layer, f"xpre{layer}")
                for k in range(POOLED[f"xa{layer}"]):
                    square_sum(f"xa{layer}", k, sq)
                residual_sums(3 * layer + 1, f"fpre{layer}")
                wait_added(pool, 3 * layer + 1, 0)
                wait_added(pool, 3 * layer + 1, KT - 1)
                nc.gpsimd.memset(y_sb[:, :, :], 0.0).then_inc(y_cleared, 1)
                for k in range(POOLED[f"ff{layer}"]):
                    square_sum(f"ff{layer}", k, sq)
                residual_sums(3 * layer + 2, "pre1" if layer == 0 else None)
                if layer == 0:
                    for name in ("qkv1a", "qkv1b"):
                        u = UNITS[name]

                        def rope_sums(kind, g, ii):
                            for m in range(HALF):
                                rope_sum(banks_out(u + kind, m, ii), (u + kind) % 2,
                                         (k1 if kind % 2 else q1)[:, g, m, :], m)

                        rope_sums(0, slice(0, 1), 0)
                        with pool.Fori(0, GROUPS - 1) as g:
                            rope_sums(1, bass.ds(g, 1), g)
                            rope_sums(2, bass.ds(g + 1, 1), g)
                        rope_sums(2 * GROUPS - 1, slice(GROUPS - 1, GROUPS), 0)

        @block.scalar
        def _(act):
            def heads_of(g, ii=0):
                act.wait_ge(raw_loaded[g % 4], ii * 32 + 16 * (g // 4 + 1))
                if g >= 2:
                    v, j = divmod(g - 2, 4)
                    if j < 3:
                        act.wait_ge(pair_used, ii * 6 + (3 * v + j + 1))
                    else:
                        act.wait_ge(bank_done, ii * 8 + 4 * (v + 1))
                nc.scalar.activation(w_hi[:, g % 2], raw[:, g % 4], ACT.Copy).then_inc(w_hi_ready, 1)

            def unit(u, bank=None, ii=0, nb=4, between=None, done=2,
                     second=2, tables_of=None, first_steps=None):
                for j in range(2):
                    if 2 + j >= done:
                        heads_of(4 * u + 2 + j, ii)
                    if between:
                        between(j)
                for m in range(5):
                    if m == 0 and u + 1 < TOTAL_UNITS:
                        heads_of(4 * u + 4, ii)
                    if m == 0 and tables_of is not None:
                        sines(tables_of)
                    if m == second and u + 1 < TOTAL_UNITS:
                        heads_of(4 * u + 5, ii)
                    if first_steps and m < first_steps[2]:
                        attention(first_steps[0], first_steps[1], m)
                    if bank and m < nb:
                        bank(m)
                    if between and m in (1, 3):
                        between(2 + m // 2)

            def copies(u, dst, nb=4, width=NB, scale=None, squares_at=None, between=None, second=2, first_steps=None):
                def bank(m):
                    src = ps[:, 4 * (u % 2) + m, 0:width]
                    act.wait_ge(bank_done, 4 * u + (m + 1) * (4 // nb))
                    if squares_at is not None:
                        nc.scalar.activation(sq[:, squares_at + m, 0:width], src, ACT.Square).then_inc(sq_ready, 1)
                    nc.scalar.activation(dst(m), src, ACT.Copy, scale=scale(m) if scale else 1.0
                                         ).then_inc(bank_out[u % 2], 4 // nb)
                unit(u, bank, nb=nb, between=between, second=second, first_steps=first_steps)

            def root(name, width=S):
                n = STATS[name]
                act.wait_ge(stat_done, n + 1)
                nc.scalar.activation(rstd[:, 0:width], ps[:, stat_bank(name), 0:width], ACT.Ln,
                                     bias=eps[:, 0:1], scale=1.0 / D).then_inc(ln_done, 1)
                act.wait_ge(ln_done, n + 1)
                nc.scalar.activation(rstd[:, 0:width], rstd[:, 0:width], ACT.Exp,
                                     scale=-0.5).then_inc(rstd_ready, 1)

            def staged_head(name, k, dst, width=S):
                act.wait_ge(staged, STAGED[name] + k + 1)
                nc.scalar.activation(dst[:, k, :], stage[:, k % 2, 0:width], ACT.Copy).then_inc(hi_ready, 1)

            def renew(name, k, x_new):
                if k is not None and 0 <= k < KT:
                    x_new(k)
                    staged_head(name, k, act_hi)
                    nc.scalar.activation(sq[:, k, :], x_sb[:, k, :], ACT.Square).then_inc(sq_ready, 1)

            def post_norm(post):
                return lambda k: wait_added(act, post, k)

            def boundary(name, post, u):
                for k in range(KT):
                    renew(name, k, post_norm(post))
                    if k == BOUNDARY_TILES:
                        heads_of(4 * u + 2)

            def copy_columns(first_unit, n):
                act.wait_ge(cols_done, n)
                nc.scalar.activation(rstd_cols[:, :], ps[:, 4 * (first_unit % 2) + 3, 0:2 * DIL],
                                     ACT.Copy).then_inc(cols_read, 1)
                act.wait_ge(cols_read, n)

            def sines(layer):
                source = angles_sb if layer else y_sb
                act.wait_ge(angles, 2 * layer + 1)
                s = C_SIGN1 if layer else C_SIGN0
                nc.scalar.activation(sin_sb[:, 0, :], source[:, 2, :], ACT.Sin, scale=cst[:, s:s + 1]).then_inc(tables, 1)
                act.wait_ge(angles, 2 * layer + 2)
                nc.scalar.activation(cos_sb[:, 0, :], source[:, 3, :], ACT.Sin).then_inc(tables, 1)
                nc.scalar.preload_act_table_set("natural_log_exp_and_others")

            def attention(a, exp, started, *events):
                for t in range(started, a.n + max(e[0] for e in events) + 1 if events else started + 1):
                    if t < a.n:
                        act.wait_ge(a.taken, t + 1)
                        if t > a.lag:
                            act.wait_ge(a.turned, t - a.lag)
                        exp(a, t)
                    if a.lag <= t < a.n + a.lag:
                        n = t - a.lag
                        act.wait_ge(a.turned, n + 1)
                        if n >= 2:
                            act.wait_ge(a.weighed, n - 1)
                        nc.scalar.activation(a.p[:, n % 2, 0:a.blocks * P], a.turned_all(n),
                                             ACT.Copy).then_inc(a.pT, 1)
                    for after, event in events:
                        h, off = divmod(t - after, a.steps)
                        if off == 0 and 1 <= h <= a.heads:
                            event(a, h - 1)

            def exp_diff(a, t):
                for c in range(2):
                    nc.scalar.activation(a.e[:, t % (a.lag + 1), c * S:(c + 1) * S], ps[:, a.score_bank(t) + c, :], ACT.Exp,
                                         bias=small[:, t % 2, 2 + c:3 + c],
                                         accum_out=small[:, t % 2, 4 + c:5 + c]).then_inc(a.exps, 1)

            def exp_cross(a, t):
                nc.scalar.activation(a.e[:, t % (a.lag + 1), 0:MEM], a.narrow_scores(t), ACT.Exp,
                                     bias=small[:, t % 2, 2:3],
                                     accum_out=small[:, t % 2, 4:5]).then_inc(a.exps, 1)

            def exp_dilated(a, t):
                w = a.blocks * P
                nc.scalar.activation(a.e[:, t % 3, 0:w], a.e[:, t % 3, 0:w], ACT.Exp,
                                     bias=small[:, t % 2, 2:3], scale=-1.0,
                                     accum_out=small[:, t % 2, 4:5]).then_inc(a.exps, 1)

            def by_token(ap):
                return ap.rearrange("p (l r) -> p r l", r=DIL)

            def by_column(ap):
                return ap.rearrange("p (r l) -> p r l", r=DIL)

            def dilated_to_y(a, h):
                act.wait_ge(a.weighed, a.steps * (h + 1))
                nc.scalar.activation(by_token(y_sb[:, h, :]), by_column(ps[:, a.out_bank(h), :]),
                                     ACT.Copy).then_inc(a.o_out, 1)

            def dilated_split(a, h):
                act.wait_ge(a.weighed, a.steps * (h + 1))
                nc.scalar.activation(by_token(act_hi[:, HALF + h, :]), by_column(ps[:, a.out_bank(h), :]),
                                     ACT.Copy).then_inc(hi_ready, 1)

            def first_half_split(k):
                def event(a, h):
                    if h == 0:
                        act.wait_ge(att_l[0].o_out, k + 1)
                        nc.scalar.activation(act_hi[:, k, :], y_sb[:, k, :], ACT.Copy).then_inc(hi_ready, 1)
                return event

            def diff_out(a, h):
                act.wait_ge(a.weighed, a.steps * (h + 1))
                if h >= 2:
                    act.wait_ge(sub_stat, h - 1)
                nc.scalar.activation(stage[:, h % 2, :], ps[:, att_d.out_bank(h), :], ACT.Square).then_inc(sub_sq, 1)
                nc.scalar.activation(y_sb[:, h, :], ps[:, att_d.out_bank(h), :], ACT.Copy).then_inc(a.o_out, 1)

            def diff_root(a, h):
                act.wait_ge(sub_stat, h + 1)
                if h >= 2:
                    act.wait_ge(sub_y, h - 1)
                nc.scalar.activation(half[:, h % 2, :], ps[:, att_d.out_bank(h), :], ACT.Ln, bias=eps[:, 0:1],
                                     scale=1.0 / P).then_inc(sub_ln, 1)
                act.wait_ge(sub_ln, h + 1)
                nc.scalar.activation(half[:, h % 2, :], half[:, h % 2, :], ACT.Exp,
                                     scale=-0.5).then_inc(sub_rstd, 1)

            def diff_head(a, h):
                act.wait_ge(sub_y, h + 1)
                nc.scalar.activation(act_hi[:, h, :], y_sb[:, h, :], ACT.Copy).then_inc(hi_ready, 1)

            def head_split(a, h):
                act.wait_ge(a.weighed, a.steps * (h + 1))
                for b in range(XB):
                    nc.scalar.activation(act_hi[:, XB * h + b, :], ps[:, a.cross_bank(XB * h + b), :], ACT.Copy).then_inc(hi_ready, 1)

            nc.scalar.preload_act_table_set("natural_log_exp_and_others")
            heads_of(0)
            for k in range(KT):
                renew("pre0", k, lambda k: wait_loaded(act, k))
                if k == 0:
                    heads_of(1)

            u = UNITS["qkv0"]
            unit(u, lambda m: root("pre0") if m == 0 else None, second=0, tables_of=0)
            act.wait_ge(lam_sums, 2)
            nc.scalar.activation(lam_w[:, 2:4], lam_w[:, 0:2], ACT.Exp).then_inc(lam_exp, 1)
            for n in range(1, 4):
                unit(u + n)
            copy_columns(u + 4, 1)
            for n in range(2):
                copies(u + 4 + n, lambda m, n=n: v0[:, m, n * NB:(n + 1) * NB],
                       scale=lambda m: rstd_cols[:, m:m + 1], first_steps=(att_d, exp_diff, 2) if n == 1 else None)
            attention(att_d, exp_diff, 2, (2, diff_out), (5, diff_root), (7, diff_head))

            for layer in range(2):
                if layer == 1:
                    for h in range(2):
                        u = UNITS["qkv1a" if h == 0 else "qkv1b"]
                        unit(u, lambda m: root("pre1") if m == 0 and h == 0 else None,
                             **(dict(done=3, second=0) if h == 0 else {}))
                        with act.Fori(0, GROUPS - 1) as g:
                            unit(u + 1, ii=g)
                            unit(u + 2, ii=g)
                        unit(u + 2 * GROUPS - 1)
                        u += 2 * GROUPS
                        if h == 0:
                            copy_columns(u, 2)
                        for g in range(GROUPS):
                            copies(u + g, lambda m, g=g: v1[:, g, m, :],
                                   scale=lambda m, g=g: rstd_cols[:, m + (DIL if g else 0):][:, 0:1],
                                   first_steps=(att_l[h], exp_dilated, 2) if g == GROUPS - 1 else None)
                        if h == 0:
                            attention(att_l[h], exp_dilated, 2, (2, dilated_to_y))
                        else:
                            attention(att_l[h], exp_dilated, 2, (2, dilated_split),
                                      *[(k - 2, first_half_split(k)) for k in range(HALF)])

                u = UNITS[f"o{layer}"]

                def mem_squares(j):
                    if j == 0:
                        act.wait_ge(mem_loaded, 16 * (layer + 1))
                        for k in range(KT):
                            nc.scalar.activation(mem_sq[:, k, :], mem_sb[:, k, :], ACT.Square).then_inc(sq_ready, 1)
                    if j == 2:
                        root(f"mem{layer}", MEM)

                def mem_heads(j):
                    for k in (2 * j, 2 * j + 1):
                        staged_head(f"mem{layer}", k, mem_hi, MEM)

                copies(u, lambda m: y_sb[:, m, :], squares_at=0, between=mem_squares)
                copies(u + 1, lambda m: y_sb[:, 4 + m, :], squares_at=4, between=mem_heads)
                u = UNITS[f"kv{layer}"]
                def planned(at):
                    if at > 0:
                        renew(f"xpre{layer}", PLAN[at - 1][1], post_norm(3 * layer))

                for n in range(4):
                    def between(j, n=n):
                        if 4 * n + j == FIRST_PLANNED - 1:
                            root(f"mix{layer}")
                        planned(4 * n + j)
                    if n < 2:
                        copies(u + n, lambda m, n=n: xv[:, m, n * NB:(n + 1) * NB], nb=2, between=between)
                    else:
                        copies(u + n, lambda m, n=n: xk[:, 4 * (n - 2) + m, :], width=MEM, between=between)
                u = UNITS[f"xq{layer}"]

                def last_planned(j):
                    if j < 2:
                        planned(16 + j)
                    if j == 1:
                        planned(18)

                unit(u, lambda m: root(f"xpre{layer}") if m == 0 else None, between=last_planned)
                unit(u + 1, first_steps=(att_x[layer], exp_cross, 2), second=4)
                attention(att_x[layer], exp_cross, 2, (3, head_split))
                u = UNITS[f"xo{layer}"]
                for n in range(2):
                    copies(u + n, lambda m, n=n: y_sb[:, 4 * n + m, :], squares_at=4 * n, second=4 if n == 1 else 2)
                root(f"xa{layer}")
                boundary(f"fpre{layer}", 3 * layer + 1, UNITS[f"ff{layer}"])

                u, first, split = UNITS[f"ff{layer}"], STAGED[f"ff{layer}"], SPLITS[f"ff{layer}"]

                def squares_of(up, c):
                    def bank(m):
                        n = 4 * up + m
                        act.wait_ge(bank_out[(u + up) % 2], banks_out(u + up, m, c * 2))
                        act.wait_ge(hi_ready, c * KT + (split + n - 1))
                        act.wait_ge(lo_ready, c * KT + (split + n - 1))
                        nc.scalar.activation(stage[:, n % 2, :], half[:, n % 2, :], ACT.Square).then_inc(staged, 1)
                        act.wait_ge(staged, c * KT + (first + n + 1))
                        nc.scalar.activation(ff_hi[:, n, :], stage[:, n % 2, :], ACT.Copy).then_inc(hi_ready, 1)
                    return bank

                def first_bank(m):
                    if m == 0:
                        root(f"fpre{layer}")
                    squares_of(0, 0)(m)

                unit(u, first_bank, done=3, second=0)
                with act.Fori(0, CHUNKS - 1) as c:
                    unit(u + 1, squares_of(1, c), c * 2)
                    unit(u + 2, None, c * 2)
                    unit(u + 3, None, c * 2)
                    unit(u + 4, squares_of(0, c + 1), c * 2)
                v = u + 4 * (CHUNKS - 1)
                unit(v + 1, squares_of(1, CHUNKS - 1), tables_of=1 if layer == 0 else None)
                unit(v + 2)

                def y_squares(j):
                    for k in (2 * j, 2 * j + 1):
                        act.wait_ge(bank_out[(v + 2 + k // 4) % 2], banks_out(v + 2 + k // 4, k % 4))
                        nc.scalar.activation(sq[:, k, :], y_sb[:, k, :], ACT.Square).then_inc(sq_ready, 1)

                unit(v + 3, between=y_squares, second=4)
                root(f"ff{layer}")
                if layer == 0:
                    boundary("pre1", 2, UNITS["qkv1a"])

        @block.vector
        def _(dve):
            steps = 0

            def step(ins):
                nonlocal steps
                steps += 1
                ins.then_inc(dve_step, 1)
                dve.wait_ge(dve_step, steps)

            def rests_of(g, ii=0):
                dve.wait_ge(w_hi_ready, ii * 8 + (g + 1))
                nc.vector.tensor_tensor(w_lo[:, g % 2], raw[:, g % 4], w_hi[:, g % 2].bitcast(f32),
                                        ALU.subtract).then_inc(w_lo_ready, 1)

            def unit(u, bank=None, ii=0, between=None, done=2, ahead=2, second=2, first_steps=None):
                for j in range(2):
                    if 2 + j >= done:
                        rests_of(4 * u + 2 + j, ii)
                    if between:
                        between(j)
                for m in range(5):
                    if m == 0 and u + 1 < TOTAL_UNITS:
                        rests_of(4 * u + 4, ii)
                    if m == 0 and first_steps:
                        first_steps()
                    if m == second and u + 1 < TOTAL_UNITS:
                        rests_of(4 * u + 5, ii)
                    if (m == 3 and ahead == 3) or (m == 2 and ahead == 4):
                        rests_of(4 * u + 6, ii)
                    if m == 3 and ahead == 4:
                        rests_of(4 * u + 7, ii)
                    if bank and m < 4:
                        bank(m)
                    if between and m in (1, 3):
                        between(2 + m // 2)

            def rope_banks(u, dst, n0, swap, ii=0, scaling=None, **kw):
                def bank(m):
                    if m == 0 and scaling:
                        scaling()
                    src = ps[:, 4 * (u % 2) + m:4 * (u % 2) + m + 1, :]
                    dve.wait_ge(bank_done, ii * 8 + (4 * u + m + 1))
                    nc.vector.tensor_tensor(dst(m), src, cos_sb[:, :, :], ALU.mult)
                    if n0 + m >= 2:
                        dve.wait_ge(rope_done, ii * 8 + (n0 + m - 1))
                    for at in range(0, P, swap):
                        to = at ^ swap
                        last = nc.vector.tensor_tensor(half[to:to + swap, m % 2:m % 2 + 1, :],
                                                       src[at:at + swap], sin_sb[at:at + swap], ALU.mult)
                    last.then_inc(bank_out[u % 2], 1)
                unit(u, bank, ii, **kw)

            def rest(name, k, dst_lo, hi, source):
                dve.wait_ge(hi_ready, SPLITS[name] + k + 1)
                nc.vector.tensor_tensor(dst_lo, source, hi.bitcast(f32), ALU.subtract).then_inc(lo_ready, 1)

            def stage_free(name, k):
                n = SPLITS[name] + k - 1
                if n > 0:
                    dve.wait_ge(hi_ready, n)
                    dve.wait_ge(lo_ready, n)

            def mem_tile(layer, i):
                name = f"mem{layer}"
                if i < KT:
                    stage_free(name, i)
                    nc.vector.scalar_tensor_tensor(stage[:, i % 2, 0:MEM], mem_sb[:, i, :], gcol(layer, "mem_g", i),
                                                   rstd[:, 0:MEM], ALU.mult, ALU.mult).then_inc(staged, 1)
                if i >= 1:
                    dve.wait_ge(staged, STAGED[name] + i)
                    rest(name, i - 1, mem_lo[:, i - 1, :], mem_hi[:, i - 1, :], stage[:, (i - 1) % 2, 0:MEM])

            def post_normed(post, layer, gains_name, i):
                nc.vector.scalar_tensor_tensor(y_sb[:, i, :], y_sb[:, i, :], gcol(layer, gains_name, i),
                                               rstd[:, :], ALU.mult, ALU.mult).then_inc(y_scaled, 1)
                if i in ADDED_BY_DVE[post]:
                    dve.wait_ge(y_scaled, KT * post + i + 1)
                    nc.vector.tensor_tensor(x_sb[:, i, :], x_sb[:, i, :], y_sb[:, i, :],
                                            ALU.add).then_inc(x_ready_dve, 1)

            def staged_x(name, layer, gains_name, k, x_new):
                x_new(k)
                stage_free(name, k)
                nc.vector.tensor_scalar(stage[:, k % 2, :], x_sb[:, k, :], gcol(layer, gains_name, k), None,
                                        ALU.mult).then_inc(staged, 1)

            def staged_rest(name, k):
                dve.wait_ge(staged, STAGED[name] + k + 1)
                rest(name, k, act_lo[:, k, :], act_hi[:, k, :], stage[:, k % 2, :])

            def renew(post, layer, gains_name, i, name=None, next_layer=None, next_gains=None, s=None):
                if i is not None:
                    post_normed(post, layer, gains_name, i)
                if s is not None and s < KT:
                    staged_x(name, next_layer, next_gains, s, x_added(post))
                if s is not None and s >= 1:
                    staged_rest(name, s - 1)

            def boundary(post, layer, gains_name, name, next_layer, next_gains, u):
                def normed(i):
                    if i < KT:
                        post_normed(post, layer, gains_name, i)

                def staged_tile(k):
                    if k < KT:
                        staged_x(name, next_layer, next_gains, k, x_added(post))

                normed(0)
                staged_tile(0)
                normed(1)
                staged_rest(name, 0)
                normed(2)
                staged_tile(1)
                normed(3)
                for k in range(1, KT):
                    staged_tile(k + 1)
                    staged_rest(name, k)
                    normed(k + 3)
                    if k == BOUNDARY_TILES - 1:
                        rests_of(4 * u + 2)

            def x_added(post):
                return lambda k: wait_added(dve, post, k)

            scalings = 0

            def scale_tables(layer, factor):
                nonlocal scalings
                dve.wait_ge(rstd_ready, STATS[f"pre{layer}"] + 1)
                dve.wait_ge(tables, 2 * layer + 2)
                for table in (cos_sb, sin_sb):
                    nc.vector.scalar_tensor_tensor(table[:, 0, :], table[:, 0, :], factor, rstd[:, :],
                                                   ALU.mult, ALU.mult).then_inc(tables_scaled, 1)
                scalings += 2
                dve.wait_ge(tables_scaled, scalings)

            def unscale_tables(factor):
                nonlocal scalings
                last_query = UNITS["qkv0"] + 1
                dve.wait_ge(bank_out[last_query % 2], banks_out(last_query, 3))
                for table in (cos_sb, sin_sb):
                    nc.vector.tensor_scalar(table[:, 0, :], table[:, 0, :], factor, None,
                                            ALU.mult).then_inc(tables_scaled, 1)
                scalings += 2
                dve.wait_ge(tables_scaled, scalings)

            def whole_turns(layer):
                inv = C_INV1 if layer else C_INV0
                angle, turns = [(angles_sb if layer else y_sb)[:, n, :] for n in range(2)]
                step(nc.vector.tensor_scalar(angle, posf[:, :], cst[:, inv:inv + 1], None, ALU.mult))
                step(nc.vector.tensor_scalar(turns, angle, 1.0 / (2 * math.pi), None, ALU.mult))
                step(nc.vector.tensor_scalar(turns, turns, 12582912.0, None, ALU.add))
                step(nc.vector.tensor_scalar(turns, turns, -12582912.0, None, ALU.add))

            def reduced_angles(layer):
                angle, turns, r, cosine = [(angles_sb if layer else y_sb)[:, n, :] for n in range(4)]
                for part in two_pi_parts():
                    step(nc.vector.scalar_tensor_tensor(angle, turns, -part, angle, ALU.mult, ALU.add))
                nc.vector.tensor_scalar(r, angle, 3.1415925, -3.1415925, ALU.min, ALU.max).then_inc(angles, 1)
                dve.wait_ge(angles, 2 * layer + 1)
                step(nc.vector.scalar_tensor_tensor(turns, r, -1.0, r, ALU.mult, ALU.max))
                nc.vector.tensor_scalar(cosine, turns, -1.0, math.pi / 2, ALU.mult, ALU.add).then_inc(angles, 1)

            def attention(a, take, probs, steps, *events):
                def mid(ins):
                    a.mids += 1
                    ins.then_inc(a.mid, 1)
                    dve.wait_ge(a.mid, a.mids)

                for t in steps:
                    if t < a.n:
                        dve.wait_ge(a.scores, t + 1)
                        take(a, t, mid)
                    if 1 <= t <= a.n:
                        probs(a, t - 1, mid)
                    for after, event in events:
                        h, off = divmod(t - after, a.steps)
                        if off == 0 and 1 <= h <= a.heads:
                            event(h - 1)

            def take_max(a, t, mid):
                if a.narrow:
                    scores, count = a.narrow_scores(t), 1
                else:
                    scores, count = ps[:, a.score_bank(t):a.score_bank(t) + 2, :], 2
                nc.vector.tensor_reduce(small[:, t % 2, 2:2 + count], scores, AX.X, ALU.max,
                                        negate=True).then_inc(a.taken, 1)

            def take_masked(a, t, mid):
                if t >= 3:
                    dve.wait_ge(a.turned, t - 2)
                w, b = a.blocks * P, a.score_bank(t)
                nc.vector.tensor_tensor_reduce(
                    out=a.e[:, t % 3, 0:w], in0=ps[:, b:b + 2, :].rearrange("p b c -> p (b c)")[:, 0:w],
                    in1=mask[:, t % DIL, :], scale=-DB_DH ** -0.5, scalar=3.0e38, op0=ALU.add, op1=ALU.min,
                    accum_out=small[:, t % 2, 2:3]).then_inc(a.taken, 1)

            def probs_plain(a, t, mid):
                dve.wait_ge(a.exps, t + 1)
                mid(nc.vector.reciprocal(small[:, t % 2, 6:7], small[:, t % 2, 4:5]))
                e = a.e[:, t % (a.lag + 1), 0:a.blocks * P]
                nc.vector.tensor_scalar(e, e, small[:, t % 2, 6:7], None, ALU.mult).then_inc(a.probs, 1)

            def probs_diff(a, t, mid):
                s = small[:, t % 2]
                e = a.e[:, t % 3]
                dve.wait_ge(a.exps, 2 * t + 2)
                mid(nc.vector.reciprocal(s[:, 6:8], s[:, 4:6]))
                mid(nc.vector.tensor_scalar(e[:, S:2 * S], e[:, S:2 * S], s[:, 7:8], lam_w[:, 5:6], ALU.mult, ALU.mult))
                nc.vector.scalar_tensor_tensor(e[:, 0:S], e[:, 0:S], s[:, 6:7], e[:, S:2 * S], ALU.mult,
                                               ALU.add).then_inc(a.probs, 1)

            dve.wait_ge(gain_loaded, 16)
            def x_is_loaded(k):
                wait_loaded(dve, k)

            staged_x("pre0", 0, "mix_pre_g", 0, x_is_loaded)
            rests_of(0)
            for k in range(KT):
                if k + 1 < KT:
                    staged_x("pre0", 0, "mix_pre_g", k + 1, x_is_loaded)
                staged_rest("pre0", k)
                if k == 1:
                    rests_of(1)

            def angles_between(layer):
                def between(j):
                    if j == 0:
                        if layer == 0:
                            prepare()
                        whole_turns(layer)
                    if j == 1:
                        reduced_angles(layer)
                return between

            def prepare():
                nonlocal steps
                dve.wait_ge(small_loaded, 64)
                nc.vector.tensor_copy(posf[:, :], half[:, 0, :].bitcast(i32)).then_inc(dve_step, 1)
                steps += 1
                nc.vector.tensor_scalar(subg[:, 1:2], subg[:, 0:1], 1.0 - LAMBDA_INIT, None, ALU.mult)
                step(nc.vector.tensor_tensor(lam_sb[:, 0, :], lam_sb[:, 0, :], lam_sb[:, 1, :], ALU.mult))
                step(nc.vector.tensor_tensor(lam_sb[:, 2, :], lam_sb[:, 2, :], lam_sb[:, 3, :], ALU.mult))
                for n in range(2):
                    nc.vector.tensor_reduce(lam_w[:, n:n + 1], lam_sb[:, 2 * n, :], AX.X, ALU.add).then_inc(lam_sums, 1)
                dve.wait_ge(constants, 4)
                step(nc.vector.tensor_reduce(phase4[:, :], ident[:, :].rearrange("p (a b) -> p b a", b=DIL), AX.X, ALU.add))
                nc.vector.tensor_scalar(phase4[:, :], phase4[:, :], -MASKED, MASKED, ALU.mult,
                                        ALU.add).then_inc(phase_ready, 1)

            u = UNITS["qkv0"]
            scalings_at = {0: lambda: scale_tables(0, DA_DQ ** -0.5), 2: lambda: unscale_tables(DA_DQ ** 0.5)}
            for n in range(4):
                dst = q0 if n < 2 else k0
                rope_banks(u + n, lambda m, dst=dst, n=n: dst[:, 4 * (n % 2) + m:4 * (n % 2) + m + 1, :],
                           4 * n, DA_DQ // 2, scaling=scalings_at.get(n), done=(2, 4, 3, 3)[n], ahead=3 if n else 4,
                           second=2 if n else 0, between=angles_between(0) if n == 0 else None)
            unit(u + 4, done=3)
            dve.wait_ge(lam_exp, 1)
            step(nc.vector.tensor_tensor(lam_w[:, 4:5], lam_w[:, 3:4], lam_w[:, 2:3], ALU.subtract))
            step(nc.vector.tensor_scalar(lam_w[:, 5:6], lam_w[:, 4:5], -LAMBDA_INIT, None, ALU.add))
            unit(u + 5, first_steps=lambda: attention(att_d, take_max, probs_diff, range(2)))

            def diff_scale(h):
                dve.wait_ge(sub_rstd, h + 1)
                nc.vector.scalar_tensor_tensor(y_sb[:, h, :], y_sb[:, h, :], subg[:, 1:2], half[:, h % 2, :],
                                               ALU.mult, ALU.mult).then_inc(sub_y, 1)

            def diff_rest(h):
                rest("o0", h, act_lo[:, h, :], act_hi[:, h, :], y_sb[:, h, :])

            attention(att_d, take_max, probs_diff, range(2, att_d.n + 9), (6, diff_scale), (8, diff_rest))

            def by_token(ap):
                return ap.rearrange("p (l r) -> p r l", r=DIL)

            def dilated_rest(h):
                k = HALF + h
                rest("o1", k, by_token(act_lo[:, k, :]), by_token(act_hi[:, k, :]),
                     ps[:, att_l[1].out_bank(h), :].rearrange("p (r l) -> p r l", r=DIL))

            def first_half_rest(k):
                def event(h):
                    if h == 0:
                        rest("o1", k, act_lo[:, k, :], act_hi[:, k, :], y_sb[:, k, :])
                return event

            for layer in range(2):
                if layer == 1:
                    for h in range(2):
                        u = UNITS["qkv1a" if h == 0 else "qkv1b"]
                        n0 = 16 + 8 * GROUPS * h

                        def rope(kind, g, ii, **kw):
                            rope_banks(u + kind, lambda m: (k1 if kind % 2 else q1)[:, g, m, :],
                                       n0 + 4 * kind, DB_DH // 2, ii, **kw)

                        if h == 0:
                            rope(0, slice(0, 1), 0, scaling=lambda: scale_tables(1, 1.0), done=3, second=0)
                        else:
                            rope(0, slice(0, 1), 0)
                        with dve.Fori(0, GROUPS - 1) as g:
                            rope(1, bass.ds(g, 1), g)
                            rope(2, bass.ds(g + 1, 1), g)
                        rope(2 * GROUPS - 1, slice(GROUPS - 1, GROUPS), 0)
                        a = att_l[h]
                        if h == 0:
                            dve.wait_ge(mask_step, MASK_STEPS)
                        for g in range(GROUPS):
                            unit(u + 2 * GROUPS + g, first_steps=None if g < GROUPS - 1 else
                                 lambda: attention(a, take_masked, probs_plain, range(2)))
                        if h == 0:
                            attention(a, take_masked, probs_plain, range(2, a.n + 1))
                        else:
                            attention(a, take_masked, probs_plain, range(2, a.n + 3), (2, dilated_rest),
                                      *[(k - 2, first_half_rest(k)) for k in range(HALF)])

                u = UNITS[f"o{layer}"]

                def mem_rests(j):
                    if j == 0:
                        dve.wait_ge(rstd_ready, STATS[f"mem{layer}"] + 1)
                        mem_tile(layer, 0)
                    for i in (2 * j + 1, 2 * j + 2):
                        mem_tile(layer, i)

                unit(u)
                unit(u + 1, between=mem_rests)
                u = UNITS[f"kv{layer}"]

                def planned(at):
                    i, k = PLAN[at]
                    if at == FIRST_PLANNED:
                        dve.wait_ge(rstd_ready, STATS[f"mix{layer}"] + 1)
                    renew(3 * layer, layer, "mix_post_g", i, f"xpre{layer}", layer, "xa_pre_g", k)

                for n in range(4):
                    unit(u + n, between=lambda j, n=n: planned(4 * n + j))

                def last_planned(j):
                    if j < 2:
                        planned(16 + j)
                    if j == 1:
                        planned(18)

                u = UNITS[f"xq{layer}"]
                a = att_x[layer]
                for n in range(2):
                    def queries(m, n=n):
                        if n == 0 and m == 0:
                            dve.wait_ge(rstd_ready, STATS[f"xpre{layer}"] + 1)
                        dve.wait_ge(bank_done, 4 * (u + n) + m + 1)
                        nc.vector.scalar_tensor_tensor(xq[:, 4 * n + m, :], ps[:, 4 * ((u + n) % 2) + m, :],
                                                       XA_DH ** -0.5, rstd[:, :], ALU.mult, ALU.mult
                                                       ).then_inc(bank_out[(u + n) % 2], 1)
                    unit(u + n, queries, between=last_planned if n == 0 else None, second=4 if n else 2, first_steps=None if n == 0 else
                         lambda: attention(a, take_max, probs_plain, range(2)))

                def head_rests(h):
                    for k in range(XB * h, XB * (h + 1)):
                        rest(f"xo{layer}", k, act_lo[:, k, :], act_hi[:, k, :], ps[:, a.cross_bank(k), :])

                attention(a, take_max, probs_plain, range(2, a.n + 4), (3, head_rests))
                for n in range(2):
                    unit(UNITS[f"xo{layer}"] + n)
                dve.wait_ge(rstd_ready, STATS[f"xa{layer}"] + 1)
                boundary(3 * layer + 1, layer, "xa_post_g", f"fpre{layer}", layer, "ffn_pre_g",
                         UNITS[f"ff{layer}"])

                u, first, split = UNITS[f"ff{layer}"], STAGED[f"ff{layer}"], SPLITS[f"ff{layer}"]

                def relus_of(up, c):
                    def bank(m):
                        n = 4 * up + m
                        dve.wait_ge(bank_done, c * 16 + (4 * (u + up) + m + 1))
                        dve.wait_ge(staged, c * KT + (first + n - 1))
                        nc.vector.scalar_tensor_tensor(half[:, n % 2, :], ps[:, 4 * ((u + up) % 2) + m, :], 0.0,
                                                       rstd[:, :], ALU.max, ALU.mult
                                                       ).then_inc(bank_out[(u + up) % 2], 1)
                        if n >= 1:
                            square_rest(n - 1, c)
                    return bank

                def square_rest(n, c):
                    dve.wait_ge(hi_ready, c * KT + (split + n + 1))
                    nc.vector.tensor_tensor(ff_lo[:, n, :], stage[:, n % 2, :], ff_hi[:, n, :].bitcast(f32),
                                            ALU.subtract).then_inc(lo_ready, 1)

                def share_of(down, c):
                    v = u + 2 + down

                    def bank(m):
                        tile = y_sb[:, 4 * down + m, :]
                        dve.wait_ge(bank_done, c * 16 + (4 * v + m + 1))
                        dve.wait_ge(bank_out[v % 2], banks_out(v - 2, m, c * 2))
                        nc.vector.tensor_tensor(tile, ps[:, 4 * (v % 2) + m, :], tile,
                                                ALU.add).then_inc(bank_out[v % 2], 1)
                    return bank

                def first_bank(m):
                    if m == 0:
                        dve.wait_ge(rstd_ready, STATS[f"fpre{layer}"] + 1)
                    relus_of(0, 0)(m)

                unit(u, first_bank, done=3, second=0)
                dve.wait_ge(y_cleared, layer + 1)
                with dve.Fori(0, CHUNKS - 1) as c:
                    unit(u + 1, relus_of(1, c), c * 2)
                    square_rest(KT - 1, c)
                    unit(u + 2, share_of(0, c), c * 2)
                    unit(u + 3, share_of(1, c), c * 2)
                    unit(u + 4, relus_of(0, c + 1), c * 2)
                c = CHUNKS - 1
                unit(u + 4 * c + 1, relus_of(1, c), between=angles_between(1) if layer == 0 else None)
                square_rest(KT - 1, c)
                unit(u + 4 * c + 2, share_of(0, c))
                unit(u + 4 * c + 3, share_of(1, c), second=4)
                dve.wait_ge(rstd_ready, STATS[f"ff{layer}"] + 1)
                if layer == 0:
                    boundary(2, 0, "ffn_post_g", "pre1", 1, "mix_pre_g", UNITS["qkv1a"])
                else:
                    for i in range(KT):
                        post_normed(5, 1, "ffn_post_g", i)

        @block.tensor
        def _(pe):
            def unit(u, hi, lo, split, ii=0, split_ii=0, tokens=None, nb=4, width=NB, last_bank=None, before_pair={},
                     early=False):
                s = 4 * (u % 2)
                if u >= 2:
                    pe.wait_ge(bank_out[u % 2], ii * 4 + 4 * (u // 2))
                for j in range(4):
                    if j in before_pair:
                        before_pair[j]()
                    pe.wait_ge(w_lo_ready, ii * 8 + (4 * u + j + 1))
                    for a in range(2):
                        k = 2 * j + a
                        if early and k == 0:
                            pe.wait_ge(hi_ready, split + 1)
                            for m in range(nb):
                                c = slice(m * P, (m + 1) * P)
                                if last_bank and m == 3:
                                    last_bank()
                                for weights in (w_hi, w_lo):
                                    nc.tensor.matmul(ps[:, s + m, :], weights[:, 0, 0, c], hi[:, 0],
                                                     start=(weights is w_hi), stop=False)
                        pe.wait_ge(lo_ready, split_ii * KT + (split + k + 1))
                        for m in range(nb):
                            if last_bank and k == 0 and m == 3 and not early:
                                last_bank()
                            wh, wl = w_hi[:, j % 2, a], w_lo[:, j % 2, a]
                            if tokens is None:
                                c = slice(m * P, (m + 1) * P)
                                passes = ((wl[:, c], hi[:, k]), (wh[:, c], lo[:, k]), (wh[:, c], hi[:, k]))
                            else:
                                th, tl = tokens(hi[:, k], m), tokens(lo[:, k], m)
                                passes = ((tl, wh), (th, wl), (th, wh))
                            if early and k == 0:
                                passes = passes[1:2]
                            for n, (left, right) in enumerate(passes):
                                last = nc.tensor.matmul(ps[:, s + m, 0:width], left, right,
                                                        start=(k == 0 and n == 0 and not early),
                                                        stop=(k == KT - 1 and n == 2))
                            if k == KT - 1:
                                last.then_inc(bank_done, 4 // nb)
                    if j < 3:
                        last.then_inc(pair_used, 1)

            def natural(ap, m):
                return ap[:, m * P:(m + 1) * P]

            def statistic(name, squares=sq):
                v, width, late = STAT_BEFORE[name], squares.shape[-1], list(range(POOLED[name], KT))
                if v >= 2:
                    pe.wait_ge(bank_out[v % 2], 4 * (v // 2))
                order = late[:-1] + [0] + late[-1:]
                for k in order:
                    if k:
                        pe.wait_ge(sq_ready, KT * STATS[name] + k + 1)
                    else:
                        pe.wait_ge(sq_summed, summed(name))
                    last = nc.tensor.matmul(ps[:, stat_bank(name), 0:width], ones[:, :], squares[:, k, :],
                                            start=(k == order[0]), stop=(k == order[-1]))
                last.then_inc(stat_done, 1)

            def sums_read(name):
                return lambda: pe.wait_ge(ln_done, STATS[name] + 1)

            def columns(v, n):
                pe.wait_ge(bank_out[v % 2], 4 * (v // 2))
                for j in range(2 * DIL):
                    tile = rstd[0:1, :]
                    tile = natural(tile, j) if j < DIL else residue(tile, j - DIL)
                    last = nc.tensor.matmul(ps[:, 4 * (v % 2) + 3, j:j + 1], tile, ones[0:1, 0:1],
                                            start=True, stop=True)
                last.then_inc(cols_done, 1)
                return lambda: pe.wait_ge(cols_read, n)

            def attention(steps, a, scores, scores_read, per_step, weigh, o_free, banks_free, head_stat=None):
                for t in steps:
                    if t < a.n:
                        if t >= 2:
                            pe.wait_ge(scores_read, per_step * (t - 1))
                        scores(t // a.steps, t % a.steps, t).then_inc(a.scores, 1)
                    if a.lag <= t < a.n + a.lag:
                        n = t - a.lag
                        if n == 0:
                            banks_free()
                        pe.wait_ge(a.probs, n + 1)
                        copied = n if a.single else n - 1
                        if copied > 0:
                            pe.wait_ge(a.pT, copied)
                        for b in range(a.blocks):
                            last = nc.tensor.transpose(a.turn_banks(n, b),
                                                       a.e[:, n % (a.lag + 1), b * P:(b + 1) * P], ident[:, :])
                        last.then_inc(a.turned, 1)
                    if a.lag < t <= a.n + a.lag:
                        n = t - a.lag - 1
                        pe.wait_ge(a.pT, n + 1)
                        if n % a.steps == 0:
                            o_free(n // a.steps)
                        weigh(n // a.steps, n % a.steps, n).then_inc(a.weighed, 1)
                    h, off = divmod(t - 4, a.steps)
                    if head_stat and off == 0 and 1 <= h <= a.heads:
                        head_stat(h - 1)

            def o_read(read):
                def o_free(h):
                    if h >= 2:
                        pe.wait_ge(read, h - 1)
                return o_free

            def p_of(a, n, b):
                return a.p[:, n % 2, b * P:(b + 1) * P]

            pe.wait_ge(constants, 4)
            u = UNITS["qkv0"]
            for n in range(4):
                if n == 1:
                    statistic("pre0")
                unit(u + n, act_hi, act_lo, SPLITS["pre0"], last_bank=sums_read("pre0") if n == 1 else None,
                     early=(n == 0))
            pe.wait_ge(rstd_ready, STATS["pre0"] + 1)
            read = columns(u + 4, 1)
            unit(u + 4, act_hi, act_lo, SPLITS["pre0"], tokens=natural, last_bank=read)

            def scores_diff(h, s, t):
                for c in range(2):
                    r = slice(c * DA_DQ, (c + 1) * DA_DQ)
                    last = nc.tensor.matmul(ps[:, 2 * (t % 2) + c, :], q0[r, h, s * P:(s + 1) * P], k0[r, h, :],
                                            start=True, stop=True)
                return last

            def weigh_diff(h, s, n):
                for b in range(S // P):
                    last = nc.tensor.matmul(ps[:, att_d.out_bank(h), s * P:(s + 1) * P], v0[:, b, h * P:(h + 1) * P],
                                            p_of(att_d, n, b), start=(b == 0), stop=(b == S // P - 1))
                return last

            def head_stat(h):
                pe.wait_ge(sub_sq, h + 1)
                pe.wait_ge(att_d.o_out, h + 1)
                nc.tensor.matmul(ps[:, att_d.out_bank(h), :], ones[:, :], stage[:, h % 2, :], start=True,
                                 stop=True).then_inc(sub_stat, 1)

            def values_out():
                last_v = UNITS["qkv0"] + 5
                pe.wait_ge(bank_out[last_v % 2], banks_out(last_v, 3))

            diff = (att_d, scores_diff, att_d.exps, 2, weigh_diff, o_read(sub_ln), values_out, head_stat)

            def diff_starts():
                pe.wait_ge(rope_done, 16)
                pe.wait_ge(bank_out[(u + 4) % 2], banks_out(u + 4, 3))
                attention(range(2), *diff)

            unit(u + 5, act_hi, act_lo, SPLITS["pre0"], tokens=natural, before_pair={3: diff_starts})
            attention(range(2, att_d.n + 1), *diff)
            pe.wait_ge(att_d.exps, 2 * att_d.n)

            def mixer_ends():
                attention(range(att_d.n + 1, att_d.n + 5), *diff)

            for layer in range(2):
                if layer == 1:
                    split = SPLITS["pre1"]
                    for h in range(2):
                        u = UNITS["qkv1a" if h == 0 else "qkv1b"]
                        if h == 0:
                            unit(u, act_hi, act_lo, split, last_bank=sums_read("ff0"), early=True)
                            statistic("pre1")
                        else:
                            unit(u, act_hi, act_lo, split, before_pair={1: mixer_ends})
                            pe.wait_ge(att_l[0].o_out, HALF)
                        with pe.Fori(0, GROUPS - 1) as g:
                            unit(u + 1, act_hi, act_lo, split, g, last_bank=sums_read("pre1"))
                            unit(u + 2, act_hi, act_lo, split, g)
                        unit(u + 2 * GROUPS - 1, act_hi, act_lo, split)
                        read = columns(u + 2 * GROUPS, 2) if h == 0 else None
                        u += 2 * GROUPS
                        for g in range(GROUPS - 1):
                            unit(u + g, act_hi, act_lo, split, tokens=natural if g == 0 else residue,
                                 last_bank=read if g == 0 else None)
                        last_v = u + GROUPS - 1
                        a = att_l[h]

                        def scores_dilated(h, r, t):
                            b = a.score_bank(t)
                            nc.tensor.matmul(ps[:, b, :], residue(q1[:, 0, h, :], r), k1[:, 0, h, :],
                                             start=True, stop=True)
                            for g in (1, 2):
                                last = nc.tensor.matmul(ps[:, b + 1, (g - 1) * P:g * P], residue(q1[:, g, h, :], r),
                                                        residue(k1[:, g, h, :], r), start=True, stop=True)
                            return last

                        def weigh_dilated(h, r, n):
                            for b in range(S // P + 2):
                                g, tile = (0, b) if b < S // P else (b - S // P + 1, r)
                                last = nc.tensor.matmul(ps[:, a.out_bank(h), r * P:(r + 1) * P],
                                                        v1[:, g, tile, h * P:(h + 1) * P], p_of(a, n, b),
                                                        start=(b == 0), stop=(b == S // P + 1))
                            return last

                        def o_split(head):
                            if head >= 2:
                                pe.wait_ge(lo_ready, SPLITS["o1"] + HALF + head - 1)

                        def values_out():
                            pe.wait_ge(bank_out[last_v % 2], banks_out(last_v, 3))

                        dilated = (a, scores_dilated, a.taken, 1, weigh_dilated,
                                   o_read(a.o_out) if h == 0 else o_split, values_out)

                        def dilated_starts():
                            pe.wait_ge(rope_done, 16 + 8 * GROUPS * (h + 1))
                            pe.wait_ge(bank_out[(last_v - 1) % 2], banks_out(last_v - 1, 3))
                            attention(range(2), *dilated)

                        unit(last_v, act_hi, act_lo, split, tokens=residue, before_pair={3: dilated_starts})
                        attention(range(2, a.n + 1), *dilated)
                        pe.wait_ge(a.taken, a.n)
                        mixer_ends = lambda dilated=dilated: attention(range(a.n + 1, a.n + 5), *dilated)

                o = UNITS[f"o{layer}"]
                split = SPLITS[f"o{layer}"]
                unit(o, act_hi, act_lo, split,
                     before_pair={1: mixer_ends, 3: lambda: statistic(f"mem{layer}", squares=mem_sq)})
                unit(o + 1, act_hi, act_lo, split, last_bank=sums_read(f"mem{layer}"))
                u = UNITS[f"kv{layer}"]
                split = SPLITS[f"mem{layer}"]
                for n in range(2):
                    unit(u + n, mem_hi, mem_lo, split, tokens=natural, nb=2,
                         before_pair={2: lambda: statistic(f"mix{layer}")} if n == 0 else {})
                for n in range(2, 4):
                    unit(u + n, mem_hi, mem_lo, split, width=MEM, last_bank=sums_read(f"mix{layer}"))
                u = UNITS[f"xq{layer}"]
                unit(u, act_hi, act_lo, SPLITS[f"xpre{layer}"], before_pair={3: lambda: statistic(f"xpre{layer}")})

                def scores_cross(h, s, t):
                    v, m = divmod(XB * h + XB - 1, 4)
                    pe.wait_ge(bank_out[(u + v) % 2], banks_out(u + v, m))
                    for b in range(XB):
                        last = nc.tensor.matmul(a.narrow_scores(t), xq[:, XB * h + b, s * P:(s + 1) * P],
                                                xk[:, XB * h + b, :], start=(b == 0), stop=(b == XB - 1))
                    return last

                def weigh_cross(h, s, n):
                    for d in range(XB):
                        for b in range(MEM // P):
                            c = (XB * h + d) * P
                            last = nc.tensor.matmul(ps[:, a.cross_bank(XB * h + d), s * P:(s + 1) * P], xv[:, b, c:c + P], p_of(a, n, b),
                                                    start=(b == 0), stop=(b == MEM // P - 1))
                    return last

                def split_read(h):
                    if h >= 2:
                        pe.wait_ge(lo_ready, SPLITS[f"xo{layer}"] + XB * (h - 1))

                def queries_out():
                    pe.wait_ge(bank_out[(u + 1) % 2], banks_out(u + 1, 3))

                a = att_x[layer]
                cross = (a, scores_cross, a.exps, 1, weigh_cross, split_read, queries_out)

                def cross_starts():
                    for n in range(4):
                        v = UNITS[f"kv{layer}"] + n
                        pe.wait_ge(bank_out[v % 2], banks_out(v, 3))
                    attention(range(2), *cross)

                unit(u + 1, act_hi, act_lo, SPLITS[f"xpre{layer}"], last_bank=sums_read(f"xpre{layer}"),
                     before_pair={3: cross_starts})
                attention(range(2, a.n + 1), *cross)
                xo = UNITS[f"xo{layer}"]
                pe.wait_ge(a.exps, a.n)
                pe.wait_ge(lo_ready, SPLITS[f"xo{layer}"] + XB * (XA_HEADS - 1))
                unit(xo, act_hi, act_lo, SPLITS[f"xo{layer}"],
                     before_pair={1: lambda: attention(range(a.n + 1, a.n + 6), *cross)})
                unit(xo + 1, act_hi, act_lo, SPLITS[f"xo{layer}"])
                statistic(f"xa{layer}")

                u = UNITS[f"ff{layer}"]
                up = (act_hi, act_lo, SPLITS[f"fpre{layer}"])
                down = (ff_hi, ff_lo, SPLITS[f"ff{layer}"])
                unit(u, *up, last_bank=sums_read(f"xa{layer}"), early=True)
                statistic(f"fpre{layer}")
                with pe.Fori(0, CHUNKS - 1) as c:
                    unit(u + 1, *up, c * 2, last_bank=sums_read(f"fpre{layer}"))
                    unit(u + 2, *down, c * 2, split_ii=c)
                    unit(u + 3, *down, c * 2, split_ii=c)
                    unit(u + 4, *up, c * 2)
                c = CHUNKS - 1
                unit(u + 4 * c + 1, *up)
                unit(u + 2, *down, c * 2, split_ii=c)
                unit(u + 3, *down, c * 2, split_ii=c)
                statistic(f"ff{layer}")


MASK_STEPS = 1 + DIL * 6


def kernel(**inputs):
    import concourse.bacc as _bacc
    from concourse.bass_utils import run_bass_kernel_spmd as _run

    def lay(a, features=True):
        return np.ascontiguousarray(a.T.reshape(-1, P, a.shape[0]).transpose(1, 0, 2))

    a = {name: np.asarray(value) for name, value in inputs.items()}
    gains = np.stack([a[name][layer] for layer in range(2) for name in LAYER_GAINS])
    arrays = {
        "x": lay(a["x"][0]),
        "mem": lay(a["mem"][0]),
        "positions": np.ascontiguousarray(a["positions"]),
        "gains": np.ascontiguousarray(gains.reshape(len(gains), KT, P).transpose(2, 0, 1)),
        "consts": rope_columns(),
        "lam": np.ascontiguousarray(a["da_lambda"].reshape(1, -1)),
        "subln_g": np.ascontiguousarray(a["da_subln_g"].reshape(P, 1)),
        "da_w_qkv": a["da_w_qkv"][0], "da_w_o": a["da_w_o"][0],
        "db_w_qkv": a["db_w_qkv"][0], "db_w_o": a["db_w_o"][0],
        "xa_wq": a["xa_wq"], "xa_wkv": a["xa_wkv"], "xa_wo": a["xa_wo"],
        "w_up": a["w_up"], "w_down": a["w_down"],
    }
    nc = _bacc.Bacc("TRN2", target_bir_lowering=False, num_devices=1)
    aps = {}
    for name, value in arrays.items():
        aps[name] = nc.dram_tensor(f"in_{name}", value.shape, mybir.dt.from_np(value.dtype), kind="ExternalInput").ap()
    out = nc.dram_tensor("out_0", (P, KT, S), mybir.dt.float32, kind="ExternalOutput").ap()
    build(nc, out=out, **aps)
    r = _run(nc, [{f"in_{name}": value for name, value in arrays.items()}], core_ids=[0])
    y = r.results[0]["out_0"]
    return np.ascontiguousarray(y.transpose(2, 1, 0).reshape(1, S, D))
```
